# Optimizing a Trainium2 kernel written in Bass

```python
import jax, jax.numpy as jnp
from jax import lax
import numpy as np

D_MODEL = 2048
BATCH = 1
SEQ = 256
DEPTH = 1
DEC_BATCH = 8
DEC_SEQ = 4
PAST_LEN = 2048
PAGE_SIZE = 128

RET_HEADS = 4
RET_DK = 256
RET_DV = 512
RET_CHUNK = 128
ROPE_BASE = 10000.0
RET_QK = RET_HEADS * RET_DK
RET_V = RET_HEADS * RET_DV
RWKV_HEADS = 16
RWKV_N = 64
RWKV_W = RWKV_HEADS * RWKV_N
DECAY_LORA = 64
AAA_LORA = 64
GATE_LORA = 160
SHIFT_W = 3 * RWKV_W + DECAY_LORA + AAA_LORA + GATE_LORA
D_FF = 5632
NORM_EPS = 1e-6
GN_EPS_RET = 1e-6
GN_EPS_RWKV = 64e-5
PROJ_W = 2 * RET_QK + 2 * RET_V + SHIFT_W + 2 * D_MODEL
Z_SPLITS = (RET_QK, 2 * RET_QK, 2 * RET_QK + RET_V, 2 * RET_QK + 2 * RET_V,
            2 * RET_QK + 2 * RET_V + SHIFT_W, 2 * RET_QK + 2 * RET_V + SHIFT_W + D_MODEL)
S_SPLITS = (RWKV_W, 2 * RWKV_W, 3 * RWKV_W, 3 * RWKV_W + DECAY_LORA, 3 * RWKV_W + DECAY_LORA + AAA_LORA)

kernel_name = "retention_rwkv7_gated_macaron_step"

def rms_norm(x, g):
    xf = x.astype(jnp.float32)
    y = xf * lax.rsqrt(jnp.mean(xf * xf, axis=-1, keepdims=True) + NORM_EPS)
    return (y * g.astype(jnp.float32)).astype(x.dtype)

def swiglu(x, w_gu, w_down):
    gate, up = jnp.split(x @ w_gu, 2, axis=-1)
    return (jax.nn.silu(gate) * up) @ w_down

def rotary(x, pos):
    half = x.shape[-1] // 2
    inv = 1.0 / (ROPE_BASE ** jnp.linspace(0.0, 1.0, half, dtype=jnp.float32))
    ang = pos[:, None] * inv[None, :]
    cos = jnp.cos(ang)[None, :, None, :]
    sin = jnp.sin(ang)[None, :, None, :]
    x1 = x[..., 0::2]
    x2 = x[..., 1::2]
    return jnp.stack([x1 * cos - x2 * sin, x1 * sin + x2 * cos], axis=-1).reshape(x.shape)

def retention_log_decay():
    return jnp.log(1.0 - 2.0 ** (-5.0 - jnp.arange(RET_HEADS, dtype=jnp.float32)))

def retention_chunk(S, q, k, v, log_g):
    C = q.shape[1]
    idx = jnp.arange(C, dtype=jnp.float32)
    rel = idx[:, None] - idx[None, :]
    mask = jnp.where(rel[None] >= 0, jnp.exp(log_g[:, None, None] * jnp.maximum(rel, 0.0)[None]), 0.0)
    scores = jnp.einsum('bihd,bjhd->bhij', q, k) * mask[None]
    inner = jnp.einsum('bhij,bjhe->bihe', scores, v)
    q_dec = jnp.exp(log_g[None, :] * (idx[:, None] + 1.0))
    cross = jnp.einsum('bihd,bhde->bihe', q, S) * q_dec[None, :, :, None]
    k_dec = jnp.exp(log_g[None, :] * (C - 1.0 - idx[:, None]))
    S_new = (jnp.exp(log_g * C)[None, :, None, None] * S
             + jnp.einsum('bjhd,bjhe->bhde', k * k_dec[None, :, :, None], v))
    return S_new, inner + cross

def retention(q, k, v, S0):
    B, T, H, _ = q.shape
    C = RET_CHUNK if T % RET_CHUNK == 0 else T
    n = T // C
    log_g = retention_log_decay()

    def to_chunks(t):
        return jnp.moveaxis(t.astype(jnp.float32).reshape(B, n, C, H, t.shape[-1]), 1, 0)

    def step(S, inp):
        qc, kc, vc = inp
        return retention_chunk(S, qc, kc, vc, log_g)

    S, o = lax.scan(step, S0.astype(jnp.float32), (to_chunks(q), to_chunks(k), to_chunks(v)))
    return S, jnp.moveaxis(o, 0, 1).reshape(B, T, H, v.shape[-1])

def retention_branch(zq, zk, zv, zg, pos, S0):
    B, T, _ = zq.shape
    q = rotary(zq.reshape(B, T, RET_HEADS, RET_DK).astype(jnp.float32), pos)
    k = rotary(zk.reshape(B, T, RET_HEADS, RET_DK).astype(jnp.float32), pos) * (RET_DK ** -0.5)
    v = zv.reshape(B, T, RET_HEADS, RET_DV)
    S, o = retention(q, k, v, S0)
    o = o * lax.rsqrt(jnp.mean(o * o, axis=-1, keepdims=True) + GN_EPS_RET)
    o = o.reshape(B, T, RET_V) * jax.nn.silu(zg.astype(jnp.float32))
    return S, o.astype(zq.dtype)

def rwkv7_recurrence(S0, r, w, k, v, a, b):
    def step(S, inp):
        rt, wt, kt, vt, at, bt = inp
        sa = jnp.einsum('bhvk,bhk->bhv', S, at)
        S = S * wt[:, :, None, :] + sa[..., None] * bt[:, :, None, :] + vt[..., None] * kt[:, :, None, :]
        return S, jnp.einsum('bhvk,bhk->bhv', S, rt)

    xs = tuple(jnp.moveaxis(t.astype(jnp.float32), 1, 0) for t in (r, w, k, v, a, b))
    S, y = lax.scan(step, S0.astype(jnp.float32), xs)
    return S, jnp.moveaxis(y, 0, 1)

def rwkv7_branch(zs, shift0, S0, p):
    B, T, _ = zs.shape
    f32 = jnp.float32
    zs_prev = jnp.concatenate([shift0[:, None, :].astype(zs.dtype), zs[:, :-1]], axis=1)
    xs = zs + (zs_prev - zs) * p['rwkv_mu']
    xr, xk, xv, xw, xa, xg = jnp.split(xs, S_SPLITS, axis=-1)

    def heads(t):
        return t.reshape(B, T, RWKV_HEADS, RWKV_N)

    w_log = -jax.nn.softplus(-(p['rwkv_w0'] + jnp.tanh(xw) @ p['rwkv_w_up']).astype(f32)) - 0.5
    decay = jnp.exp(-jnp.exp(w_log))
    a_rate = jax.nn.sigmoid((p['rwkv_a0'] + xa @ p['rwkv_a_up']).astype(f32))
    g = (jax.nn.sigmoid(xg) @ p['rwkv_g_up']).astype(f32)
    k = xk.astype(f32)
    kk = heads(k * p['rwkv_k_k'].astype(f32))
    kk = kk * lax.rsqrt(jnp.maximum(jnp.sum(kk * kk, axis=-1, keepdims=True), 1e-24))
    k = heads(k * (1.0 + (a_rate - 1.0) * p['rwkv_k_a'].astype(f32)))
    r = heads(xr.astype(f32))
    v = heads(xv.astype(f32))
    S, y = rwkv7_recurrence(S0, r, heads(decay), k, v, -kk, kk * heads(a_rate))
    mean = jnp.mean(y, axis=-1, keepdims=True)
    var = jnp.mean(jnp.square(y - mean), axis=-1, keepdims=True)
    y = ((y - mean) * lax.rsqrt(var + GN_EPS_RWKV)).reshape(B, T, RWKV_W)
    y = y * p['rwkv_ln_w'].astype(f32) + p['rwkv_ln_b'].astype(f32)
    bonus = jnp.sum(r * k * p['rwkv_r_k'].astype(f32), axis=-1, keepdims=True) * v
    y = (y + bonus.reshape(B, T, RWKV_W)) * g
    return S, y.astype(zs.dtype), zs[:, -1]

def decoder_layer(x, pos, ret_S0, rwkv_S0, shift0, p):
    x = x + 0.5 * swiglu(rms_norm(x, p['norm_ffn1']), p['ffn1_w_gu'], p['ffn1_w_down'])
    h = rms_norm(x, p['norm_mix'])
    z = h @ p['w_in']
    zq, zk, zv, zg, zs, zgr, zgw = jnp.split(z, Z_SPLITS, axis=-1)
    ret_S, o_ret = retention_branch(zq, zk, zv, zg, pos, ret_S0)
    rwkv_S, o_rwkv, shift = rwkv7_branch(zs, shift0, rwkv_S0, p)
    merged = (jax.nn.sigmoid(zgr) * (o_ret @ p['w_ret_o'])
              + jax.nn.sigmoid(zgw) * (o_rwkv @ p['w_rwkv_o']))
    x = x + merged @ p['w_out']
    x = x + 0.5 * swiglu(rms_norm(x, p['norm_ffn2']), p['ffn2_w_gu'], p['ffn2_w_down'])
    return x, ret_S, rwkv_S, shift

def run_trunk(x, pos, ret0, rwkv0, shift0, layer_params, norm_final):
    ret_out, rwkv_out, shift_out = [], [], []
    for l in range(DEPTH):
        p = {name: arr[l] for name, arr in layer_params.items()}
        x, rS, wS, sh = decoder_layer(x, pos, ret0[l], rwkv0[l], shift0[l], p)
        ret_out.append(rS)
        rwkv_out.append(wS)
        shift_out.append(sh)
    return rms_norm(x, norm_final), jnp.stack(ret_out), jnp.stack(rwkv_out), jnp.stack(shift_out)

def setup_inputs(seed: int = 0) -> dict:
    key = jax.random.key(seed)
    ks = jax.random.split(key, 32)
    f32 = jnp.float32
    L = DEPTH
    D = D_MODEL

    def nrm(k, shape, s):
        return jax.random.normal(k, shape, f32) * s

    return {
        "x_prompt": nrm(ks[0], (BATCH, SEQ, D), 1.0),
        "x_sample": nrm(ks[1], (DEC_BATCH, DEC_SEQ, D), 1.0),
        "state_ret": nrm(ks[2], (L, DEC_BATCH, RET_HEADS, RET_DK, RET_DV), 0.3),
        "state_rwkv": nrm(ks[3], (L, DEC_BATCH, RWKV_HEADS, RWKV_N, RWKV_N), 0.3),
        "state_shift": nrm(ks[4], (L, DEC_BATCH, SHIFT_W), 1.0),
        "norm_ffn1": 1.0 + nrm(ks[5], (L, D), 0.05),
        "ffn1_w_gu": nrm(ks[6], (L, D, 2 * D_FF), D ** -0.5),
        "ffn1_w_down": nrm(ks[7], (L, D_FF, D), D_FF ** -0.5),
        "norm_mix": 1.0 + nrm(ks[8], (L, D), 0.05),
        "w_in": nrm(ks[9], (L, D, PROJ_W), D ** -0.5),
        "w_ret_o": nrm(ks[10], (L, RET_V, D), RET_V ** -0.5),
        "rwkv_mu": jax.random.uniform(ks[11], (L, SHIFT_W), f32),
        "rwkv_w0": jax.random.uniform(ks[12], (L, RWKV_W), f32, -4.0, 0.0),
        "rwkv_w_up": nrm(ks[13], (L, DECAY_LORA, RWKV_W), 0.5 * DECAY_LORA ** -0.5),
        "rwkv_a0": nrm(ks[14], (L, RWKV_W), 0.5),
        "rwkv_a_up": nrm(ks[15], (L, AAA_LORA, RWKV_W), AAA_LORA ** -0.5),
        "rwkv_g_up": nrm(ks[16], (L, GATE_LORA, RWKV_W), GATE_LORA ** -0.5),
        "rwkv_k_k": 0.85 + nrm(ks[17], (L, RWKV_W), 0.05),
        "rwkv_k_a": 1.0 + nrm(ks[18], (L, RWKV_W), 0.05),
        "rwkv_r_k": nrm(ks[19], (L, RWKV_HEADS, RWKV_N), 0.1),
        "rwkv_ln_w": 1.0 + nrm(ks[20], (L, RWKV_W), 0.05),
        "rwkv_ln_b": nrm(ks[21], (L, RWKV_W), 0.01),
        "w_rwkv_o": nrm(ks[22], (L, RWKV_W, D), RWKV_W ** -0.5),
        "w_out": nrm(ks[23], (L, D, D), D ** -0.5),
        "norm_ffn2": 1.0 + nrm(ks[24], (L, D), 0.05),
        "ffn2_w_gu": nrm(ks[25], (L, D, 2 * D_FF), D ** -0.5),
        "ffn2_w_down": nrm(ks[26], (L, D_FF, D), D_FF ** -0.5),
        "norm_final": 1.0 + nrm(ks[27], (D,), 0.05),
    }

def reference(x_prompt, x_sample, state_ret, state_rwkv, state_shift,
              norm_ffn1, ffn1_w_gu, ffn1_w_down, norm_mix, w_in, w_ret_o,
              rwkv_mu, rwkv_w0, rwkv_w_up, rwkv_a0, rwkv_a_up, rwkv_g_up,
              rwkv_k_k, rwkv_k_a, rwkv_r_k, rwkv_ln_w, rwkv_ln_b, w_rwkv_o, w_out,
              norm_ffn2, ffn2_w_gu, ffn2_w_down, norm_final):
    layer_params = {
        'norm_ffn1': norm_ffn1, 'ffn1_w_gu': ffn1_w_gu, 'ffn1_w_down': ffn1_w_down,
        'norm_mix': norm_mix, 'w_in': w_in, 'w_ret_o': w_ret_o,
        'rwkv_mu': rwkv_mu, 'rwkv_w0': rwkv_w0, 'rwkv_w_up': rwkv_w_up,
        'rwkv_a0': rwkv_a0, 'rwkv_a_up': rwkv_a_up, 'rwkv_g_up': rwkv_g_up,
        'rwkv_k_k': rwkv_k_k, 'rwkv_k_a': rwkv_k_a, 'rwkv_r_k': rwkv_r_k,
        'rwkv_ln_w': rwkv_ln_w, 'rwkv_ln_b': rwkv_ln_b, 'w_rwkv_o': w_rwkv_o,
        'w_out': w_out, 'norm_ffn2': norm_ffn2, 'ffn2_w_gu': ffn2_w_gu, 'ffn2_w_down': ffn2_w_down,
    }
    Bp, Tp, _ = x_prompt.shape
    Bs, Ts, _ = x_sample.shape
    pos_p = jnp.arange(Tp, dtype=jnp.float32)
    ret0_p = jnp.zeros((DEPTH, Bp, RET_HEADS, RET_DK, RET_DV), jnp.float32)
    rwkv0_p = jnp.zeros((DEPTH, Bp, RWKV_HEADS, RWKV_N, RWKV_N), jnp.float32)
    shift0_p = jnp.zeros((DEPTH, Bp, SHIFT_W), x_prompt.dtype)
    y_prompt, ret_p, rwkv_p, shift_p = run_trunk(x_prompt, pos_p, ret0_p, rwkv0_p, shift0_p,
                                                 layer_params, norm_final)
    pos_s = PAST_LEN + jnp.arange(Ts, dtype=jnp.float32)
    y_sample, ret_s, rwkv_s, shift_s = run_trunk(x_sample, pos_s, state_ret, state_rwkv, state_shift,
                                                 layer_params, norm_final)
    return (y_prompt, y_sample, ret_p, rwkv_p, shift_p, ret_s, rwkv_s, shift_s)


_drawn_inputs = setup_inputs


def setup_inputs(seed=0):
    import zlib

    import numpy as np

    out = dict(_drawn_inputs(seed))
    spreads = {}
    factors = {'rwkv_ln_w': 4.606, 'rwkv_ln_b': 25.687, 'norm_ffn2': 3.068}
    for name, (base, spread) in spreads.items():
        noise = np.random.default_rng([zlib.crc32(name.encode()), seed]).standard_normal(out[name].shape)
        drawn = base * np.exp(spread * noise) if base else spread * noise
        out[name] = __import__('jax').numpy.asarray(drawn.astype(out[name].dtype))
    for name, factor in factors.items():
        out[name] = (out[name] * factor).astype(out[name].dtype)
    return out
```

```python
from contextlib import ExitStack

import numpy as np

import concourse.bass as bass
from concourse import mybir

F32, F32R = mybir.dt.float32, mybir.dt.float32r
ALU, ACT = mybir.AluOpType, mybir.ActivationFunctionType

P = 128
D = 2048
KT = D // P
FF = 5632
HALF = FF // 2
HT = HALF // P
SEQ, SB, ST = 256, 8, 4
NS = SB * ST
T = SEQ + NS
RH, DK, DV = 4, 256, 512
VT = DV // P
RW = 1024
PAIRS = RW // P
N = 64
CH = 64
BLK = 2048
EPS = 1e-6
GN_EPS = 64e-5
KAPPA = float(np.exp(np.float32(-0.5)))
GATE1 = 160 - P
PP = 3 * P + 3 * SB + 11
C_SHIFT = 3 * P
C_MU = C_SHIFT + 3 * SB
C_W0, C_A0, C_KK, C_KA, C_RK, C_LNW, C_LNB, C_OKA = (C_MU + 3 + n for n in range(8))
RC = 384 + NS + NS + 4
LEVELS = (2, 4, 8, 16, 32)
SLOTS = 4
LOADS, MIX_LOADS = 5, 8

RET_PE = ("v_turned", "k_turned", "scores", "kv0", "kv1", "o_prompt") + tuple(
    f"{w}{b}{e}" for b in range(SB) for w, e in (("cross", ""), ("kv_s", "e"), ("kv_s", "o"))) + ("norm",)
RET_ACT = ("v_out", "k_out", "state0", "state1", "o_prompt_out", "squared", "root")
RET_DVE = ("q_scaled", "masked", "k_owned", "o_sample_out", "done")
RW_PE = ("lora", "kk_sum", "turned", "bonus", "prod_b", "prod_k", "prod_s", "x1") + tuple(
    f"{w}{s}" for s in LEVELS for w in ("y", "d")) + ("nv", "gh") + (
    "upd0", "u1", "upd1", "u2", "upd2", "u3", "upd3", "u_s", "u_s_turned", "upd_s", "out", "mean", "var")
RW_ACT = ("gates", "square", "root", "exps", "turned_out", "eye") + tuple(f"y_out{s}" for s in LEVELS) + (
    "nv_out", "h_out", "us_out", "y_prompt_out", "y_square", "y_root")
RW_DVE = ("shifted", "summed", "kk_max", "abk", "rk", "bonus", "masked_b", "masked_k", "masked_s", "x1") + tuple(
    f"x{s}" for s in LEVELS) + (
    "g_out", "s1", "u1", "s2", "u2", "s3", "u3", "s4", "ub", "s_s", "y", "centred", "done")
RW_POOL = ("lm1",) + tuple(f"lm{s}" for s in LEVELS)


def build(nc, d):
    with ExitStack() as ctx:
        place = [-(-nc.sbuf_base // 32) * 32]

        def sb(name, shape, dt=F32, at=None):
            size = int(np.prod(shape[1:])) * 4
            offset = place[0] if at is None else at
            if at is None:
                place[0] += -(-size // 32) * 32
            return nc.alloc_sbuf_tensor_at("sb_" + name, list(shape), dt, offset=offset)

        def sem(name):
            return ctx.enter_context(nc.semaphore(name))

        psum = ctx.enter_context(nc.psum_tensor("psum", [P, 8, 512], F32))

        raw = sb("raw", [P, 2, BLK])
        w_hi = sb("w_hi", [P, 2, BLK], F32R)
        w_lo = sb("w_lo", [P, 2, BLK], F32R)
        h_hi = sb("h_hi", [P, KT, T], F32R)
        h_lo = sb("h_lo", [P, KT, T], F32R)
        mean_w = sb("mean_w", [P, P])
        head_w = sb("head_w", [P, P])
        ident = sb("ident", [P, P])
        gains = sb("gains", [P, 4, KT])
        eps_c = sb("eps_c", [P, 2])
        arena = place[0]

        x = sb("x", [P, KT, T])
        g_hi = sb("g_hi", [P, HT, T], F32R)
        g_lo = sb("g_lo", [P, HT, T], F32R)
        gate = sb("gate", [P, 2, T])
        prod = sb("prod", [P, 2, T])
        sq = sb("sq", [P, 2, T])
        scale = sb("scale", [P, T])
        ffn_end = place[0]

        place[0] = arena
        o_ret = sb("o_ret", [P, RH * VT, T])
        o_rw = sb("o_rw", [P, PAIRS, T])
        mix = place[0]
        zs = sb("zs", [P, 3, 2, 1 + SEQ + SB * (ST + 1)])
        qk = sb("qk", [P, 4, T])
        vg = sb("vg", [P, 2, VT, T])
        lora = sb("lora", [P, 3, T])
        trig = sb("trig", [P, 2, T])
        levels_m = sb("levels_m", [P, 1 + len(LEVELS), P])
        tri = sb("tri", [P, 2, P])
        tri_s = sb("tri_s", [NS, 2, NS])
        own = sb("own", [NS, SB])
        blocks_m = sb("blocks_m", [P, P])
        run_m = sb("run_m", [P, T])
        lpk = sb("lpk", [P, 3 * SB + 3])
        last = sb("last", [P, 6, 1 + SB])
        units = place[0]
        rc = sb("rc", [P, RC])
        v_tok = sb("v_tok", [P, 2, DV])
        v_tok_s = sb("v_tok_s", [NS, DV])
        k_tok = sb("k_tok", [P, 2, DK])
        k_tok_s = sb("k_tok_s", [NS, DK])
        k_own = sb("k_own", [NS, SB, DK])
        scores = sb("scores", [P, 384 + NS])
        rot = sb("rot", [P, 2, T])
        q_s = sb("q_s", [P, 2, NS])
        s_ret = sb("s_ret", [P, SLOTS, 2, DV])
        s_out = sb("s_out", [P, 2, DV])
        r_scale = sb("r_scale", [P, T])
        ret_end = place[0]
        o_T = vg[:, 0]
        o_sq = qk
        place[0] = units
        pp = sb("pp", [P, PP])
        s0 = sb("s0", [P, SB, N])
        shifted_at = place[0]
        shifted = sb("shifted", [P, 3, T])
        decays = sb("decays", [P, 3, T], at=shifted_at)
        rkv = sb("rkv", [P, 3, T])
        wag = sb("wag", [P, 3, T])
        csum = sb("csum", [P, 2, T])
        ksq = sb("ksq", [P, T])
        kn = sb("kn", [P, T])
        kk = sb("kk", [P, T])
        ar = sb("ar", [P, 2, T])
        bc = sb("bc", [P, T])
        kc = sb("kc", [P, T])
        k2 = sb("k2", [P, T])
        rk = sb("rk", [P, T])
        bonus = sb("bonus", [P, T])
        tok = sb("tok", [P, 2, 4, P])
        tok_s = sb("tok_s", [NS, 4, P])
        own_at = place[0]
        mt = sb("mt", [P, 4, P])
        nt = sb("nt", [P, 4, P])
        lm = sb("lm", [P, 4, P])
        xm = sb("xm", [P, 4, P])
        ub = sb("ub", [NS, SB, P], at=own_at)
        vb = sb("vb", [NS, SB, P], at=own_at + 4 * SB * P)
        pt = sb("pt", [P, 4, P])
        qt = sb("qt", [P, 4, P])
        xt = sb("xt", [P, 4, P])
        ym = sb("ym", [P, 4, P])
        ms = sb("ms", [NS, 4, 2, NS])
        lm_s = sb("lm_s", [NS, 2, NS])
        xm_s = sb("xm_s", [NS, 2, NS])
        xt_s = sb("xt_s", [NS, 2, NS])
        ym_s = sb("ym_s", [NS, 2, NS])
        nv = sb("nv", [P, 3, P])
        gm = sb("gm", [P, 3, P])
        hT = sb("hT", [P, 2, P])
        hr = sb("hr", [P, 2, NS])
        um = sb("um", [P, 2, P])
        um_s = sb("um_s", [NS, P])
        st = sb("st", [P, 4, P])
        stt = sb("stt", [P, P])
        us = sb("us", [P, 2, NS])
        ysb = sb("ysb", [P, T])
        yc = sb("yc", [P, T])
        rw_end = place[0]

        place[0] = mix
        or_hi = sb("or_hi", [P, RH * VT, T], F32R)
        or_lo = sb("or_lo", [P, RH * VT, T], F32R)
        part = sb("part", [P, KT, T])
        place[0] = arena
        ow_hi = sb("ow_hi", [P, PAIRS, T], F32R)
        ow_lo = sb("ow_lo", [P, PAIRS, T], F32R)
        mg_at = mix
        m_hi = sb("m_hi", [P, KT, T], F32R, at=mg_at)
        m_lo = sb("m_lo", [P, KT, T], F32R, at=mg_at + 4 * KT * T)
        gate_m = sb("gate_m", [P, 2, T], at=mix + 12 * KT * T)
        prod_m = sb("prod_m", [P, 2, T], at=mix + 12 * KT * T + 8 * T)
        assert max(ffn_end, ret_end, rw_end, mix + 12 * KT * T + 16 * T) <= nc.sbuf_usable_end

        raw_landed = [sem("raw_landed0"), sem("raw_landed1")]
        hi_made, lo_made = sem("hi_made"), sem("lo_made")
        used = sem("used")
        psum_free = [sem("psum_free0"), sem("psum_free1")]
        loaded, mix_loaded = sem("loaded"), sem("mix_loaded")
        spilled, x_back = sem("spilled"), sem("x_back")
        act_chain, dve_chain = sem("act_chain"), sem("dve_chain")
        x_made = sem("x_made")
        squares, square_used, root_made = sem("squares"), sem("square_used"), sem("root_made")
        normed, normed_hi, normed_lo = sem("normed"), sem("normed_hi"), sem("normed_lo")
        gate_made, gate_used = sem("gate_made"), sem("gate_used")
        hidden, hidden_hi, hidden_lo = sem("hidden"), sem("hidden_hi"), sem("hidden_lo")
        merged, merged_hi, merged_lo = sem("merged"), sem("merged_hi"), sem("merged_lo")
        o_hi, o_lo = sem("o_hi"), sem("o_lo")
        lora_shifted, lora_made = sem("lora_shifted"), sem("lora_made")
        last_made, last_sent = sem("last_made"), sem("last_sent")
        ret_pe, ret_act, ret_dve = sem("ret_pe"), sem("ret_act"), sem("ret_dve")
        rw_pe, rw_act, rw_dve, rw_pool = sem("rw_pe"), sem("rw_act"), sem("rw_dve"), sem("rw_pool")
        rc_landed, pp_landed = sem("rc_landed"), sem("pp_landed")
        s_landed = [sem(f"s_landed{i}") for i in range(SLOTS)]
        s_sent = [sem(f"s_sent{i}") for i in range(SLOTS)]
        s_new = sem("s_new")
        rp_sent, wp_sent, ws_sent = sem("rp_sent"), sem("wp_sent"), sem("ws_sent")
        stored = sem("stored")
        parted = sem("parted")

        def at(steps, name, unit):
            return unit * len(steps) + (steps.index(name) + 1)

        def is_first(i):
            return isinstance(i, int) and i == 0

        def wait(eng, s, value):
            if not (isinstance(value, int) and value <= 0):
                eng.wait_ge(s, value)

        def loop(eng, count, body):
            body(0)
            if count > 1:
                with eng.Fori(1, count) as i:
                    body(i)

        class Chain:

            def __init__(self, eng, s):
                self.eng, self.s, self.n, self.base = eng, s, 0, 0

            def do(self, ins, wait=True):
                ins.then_inc(self.s, 1)
                self.n += 1
                if wait:
                    self.eng.wait_ge(self.s, self.base + self.n)

            def loop(self, count, body):
                before = self.n
                body(0)
                per = self.n - before
                if count > 1:
                    with self.eng.Fori(1, count) as i:
                        self.base, self.n = i * per, before
                        body(i)
                        assert self.n - before == per, (self.n - before, per)
                    self.base, self.n = 0, before + per * count

        taken = [0, 0]

        def phase(nb, npairs, times):
            b, g = taken
            taken[0] += nb * times
            taken[1] += npairs * times
            return b, g

        ffn = []
        for n in range(2):
            if n:
                lora_ph = phase(3, 2, 1)
                mix_ph = phase(18, 10, RH)
                ret_o_ph = phase(4, 2, PAIRS)
                rw_o_ph = phase(4, 2, PAIRS)
                w_out_ph = phase(4, 2, 4)
            ffn.append([(phase(4, 2, HT // 2), phase(8, 2, 4)) for _ in range(2)])
        DOWN = HT * P // 2
        LORA2 = KT * GATE1

        def units_free_of_retention(eng, i):
            eng.wait_ge(rp_sent, i * 32 + 32)
            for s in s_sent:
                eng.wait_ge(s, i * (16 * SB // SLOTS) + 16 * SB // SLOTS)

        def units_free_of_rwkv(eng, i):
            eng.wait_ge(rw_dve, i * (2 * len(RW_DVE)) + 2 * len(RW_DVE))
            eng.wait_ge(ws_sent, i * 32 + 32)
            eng.wait_ge(wp_sent, i * 64 + 64)

        def mixing_over(eng):
            units_free_of_rwkv(eng, RH - 1)
            eng.wait_ge(last_sent, 16 * (RH + 1))

        def mixed_in(eng, i):
            for s in range(2):
                eng.wait_ge(psum_free[s], i * 5 + (mix_ph[1] // 2 + 5))

        block = ctx.enter_context(nc.Block())

        @block.sync
        def _(sp):
            def load(n, first, src, cols=BLK):
                wait(sp, lo_made, n + (first - 1))
                sp.dma_start(raw[:, first % 2, 0:cols], src).then_inc(raw_landed[first % 2], 16)

            def run(ph, times, src, widths):
                def body(i):
                    for j, cols in enumerate(widths):
                        load(i * len(widths), ph[0] + j, src[i, j, :, 0:cols], cols)
                loop(sp, times, body)

            def feed(n, gu, down):
                for f in range(2):
                    run(ffn[n][f][0], HT // 2, gu[f], [BLK] * 4)
                    run(ffn[n][f][1], 4, down[f], [DOWN] * 8)

            feed(0, d["gu1"], d["down1"])
            run(lora_ph, 1, d["w_lora"], [BLK, BLK, LORA2])
            run(mix_ph, RH, d["w_mix"], [BLK] * 18)
            run(ret_o_ph, PAIRS, d["w_ro"], [BLK] * 4)
            run(rw_o_ph, PAIRS, d["w_wo"], [BLK, BLK, BLK // 2, BLK // 2])
            run(w_out_ph, 4, d["w_out"], [BLK] * 4)
            feed(1, d["gu2"], d["down2"])
            for k in range(0, KT, 4):
                sp.wait_ge(normed, 3 * KT + k + 4)
                sp.dma_start(d["y"][:, k:k + 4, :], x[:, k:k + 4, :]).then_inc(stored, 16)
            sp.wait_ge(stored, 16 * (KT // 4))

        @block.tensor
        def _(pe):
            def products(out, wh, wl, xh, xl, start, stop):
                pe.matmul(out, wh, xh, start=start, stop=False)
                pe.matmul(out, wh, xl, start=False, stop=False)
                return pe.matmul(out, wl, xh, start=False, stop=stop)

            def pair(i, ph, j, g, nblk, nk, hi, lo, widths=(P, P), ready=None):
                b0, g0, bs, gs = ph
                pe.wait_ge(psum_free[(g0 + g) % 2], i * (gs // 2) + (g0 + g) // 2)
                per = nk * len(widths) // nblk
                u = 0
                for jj in range(j, j + nblk):
                    pe.wait_ge(lo_made, i * bs + (b0 + jj + 1))
                    slot = (b0 + jj) % 2
                    col = 0
                    for _ in range(per):
                        k, m = divmod(u, len(widths))
                        w = widths[m]
                        if ready is not None and m == 0:
                            pe.wait_ge(*ready(k))
                        mm = products(psum[0:w, 2 * ((g0 + g) % 2) + m, 0:T],
                                      w_hi[:, slot, col:col + w], w_lo[:, slot, col:col + w],
                                      hi[:, k, :], lo[:, k, :], k == 0, k == nk - 1)
                        col += w
                        u += 1
                    mm.then_inc(used, 1)

            def norm(r):
                for k in range(KT):
                    pe.wait_ge(squares, r * KT + k + 1)
                    pe.matmul(psum[:, 4, 0:T], mean_w[:, :], sq[:, k % 2, :],
                              start=(k == 0), stop=(k == KT - 1)).then_inc(square_used, 1)

            pe.wait_ge(loaded, 16 * LOADS)

            def normed_by(r):
                return lambda k: (normed_lo, r * KT + k + 1)

            def feed(n):
                norm(2 * n)
                for f in range(2):
                    up_ph, down_ph = (*ffn[n][f][0], 4, 2), (*ffn[n][f][1], 8, 2)

                    def up(i):
                        pair(i, up_ph, 0, 0, 2, KT, h_hi, h_lo, ready=normed_by(2 * n) if is_first(i) and f == 0 else None)
                        pair(i, up_ph, 2, 1, 2, KT, h_hi, h_lo)
                    loop(pe, HT // 2, up)
                    done = (2 * n + f) * (HT // 2)

                    def down(i):
                        pair(i, down_ph, 0, 0, 4, HT, g_hi, g_lo,
                             ready=(lambda k: (hidden_lo, done + k // 2 + 1)) if is_first(i) else None)
                        pair(i, down_ph, 4, 1, 4, HT, g_hi, g_lo)
                    loop(pe, 4, down)

            feed(0)
            norm(1)
            pair(0, (*lora_ph, 3, 2), 0, 0, 2, KT, h_hi, h_lo, ready=normed_by(1))
            pair(0, (*lora_ph, 3, 2), 2, 1, 1, KT, h_hi, h_lo, widths=(GATE1,))

            def projections(i):
                ph = (*mix_ph, 18, 10)
                for j in range(8):
                    pair(i, ph, 2 * j, j, 2, KT, h_hi, h_lo)
                for j in range(8, 10):
                    pair(i, ph, 8 + j, j, 1, KT, h_hi, h_lo, widths=(P,))

            def transpose(out, in_, n=P):
                return pe.transpose(out, in_, ident[0:n, 0:n])

            def retention(h):
                def step(mm):
                    mm.then_inc(ret_pe, 1)

                def after(s, steps, name):
                    pe.wait_ge(s, at(steps, name, h))
                mixed_in(pe, h)
                pe.wait_ge(rw_dve, h * (2 * len(RW_DVE)))
                for tt in range(2):
                    for m in range(VT):
                        mm = transpose(psum[:, 4 + tt, m * P:(m + 1) * P], vg[:, 0, m, tt * P:(tt + 1) * P])
                for m in range(VT):
                    mm = transpose(psum[0:NS, 6, m * P:(m + 1) * P], vg[:, 0, m, SEQ:T])
                step(mm)
                for tt in range(2):
                    for e in range(2):
                        mm = transpose(psum[:, 7, (2 * tt + e) * P:(2 * tt + e + 1) * P], qk[:, 2 + e, tt * P:(tt + 1) * P])
                after(ret_act, RET_ACT, "v_out")
                for e in range(2):
                    mm = transpose(psum[0:NS, 6, e * P:(e + 1) * P], qk[:, 2 + e, SEQ:T])
                step(mm)
                for e in range(2):
                    pe.matmul(psum[:, 4, 0:SEQ], qk[:, 2 + e, 0:P], qk[:, e, 0:SEQ], start=(e == 0), stop=(e == 1))
                for e in range(2):
                    pe.matmul(psum[:, 5, 0:P], qk[:, 2 + e, P:SEQ], qk[:, e, P:SEQ], start=(e == 0), stop=(e == 1))
                for e in range(2):
                    mm = pe.matmul(psum[0:NS, 5, P:P + NS], qk[:, 2 + e, SEQ:T], qk[:, e, SEQ:T], start=(e == 0),
                                   stop=(e == 1), skip_group_check=True)
                step(mm)
                after(ret_act, RET_ACT, "k_out")
                for e in range(2):
                    for tt in range(2):
                        mm = pe.matmul(psum[:, 6 + e, :], k_tok[:, tt, e * P:(e + 1) * P], v_tok[:, tt, :],
                                       start=(tt == 0), stop=(tt == 1))
                    step(mm)
                after(ret_dve, RET_DVE, "masked")
                for m in range(VT):
                    out = psum[:, 4 + m // 2, (m % 2) * SEQ:(m % 2 + 1) * SEQ]
                    pe.matmul(out, v_tok[:, 0, m * P:(m + 1) * P], scores[:, 0:SEQ], start=(m % 2 == 0), stop=False,
                              skip_group_check=True)
                    mm = pe.matmul(out[:, P:SEQ], v_tok[:, 1, m * P:(m + 1) * P], scores[:, SEQ:384], start=False,
                                   stop=True, skip_group_check=True)
                step(mm)
                after(ret_dve, RET_DVE, "q_scaled")
                after(ret_act, RET_ACT, "state0")
                for m in range(VT):
                    pe.matmul(psum[:, 6, m * NS:(m + 1) * NS], v_tok_s[:, m * P:(m + 1) * P], scores[0:NS, 384:384 + NS],
                              start=(m == 0), stop=False, skip_group_check=True)
                after(ret_act, RET_ACT, "state1")
                after(ret_act, RET_ACT, "o_prompt_out")
                after(ret_dve, RET_DVE, "k_owned")
                for bb in range(SB):
                    slot = bb % SLOTS
                    pe.wait_ge(s_landed[slot], h * (16 * SB // SLOTS) + 16 * (bb // SLOTS + 1))
                    for m in range(VT):
                        for e in range(2):
                            mm = pe.matmul(psum[:, 6, m * NS + bb * ST:m * NS + (bb + 1) * ST],
                                           s_ret[:, slot, e, m * P:(m + 1) * P], q_s[:, e, bb * ST:(bb + 1) * ST],
                                           start=False, stop=(e == 1), skip_group_check=True)
                    step(mm)
                    for e in range(2):
                        u = 2 * bb + e
                        if u >= 3:
                            pe.wait_ge(s_new, h * (2 * SB) + (u - 2))
                        step(pe.matmul(psum[:, (7, 4, 5)[u % 3], :], k_own[:, bb, e * P:(e + 1) * P], v_tok_s[:, :],
                                       start=True, stop=True))
                after(ret_act, RET_ACT, "squared")
                for m in range(VT):
                    mm = pe.matmul(psum[:, 7, 0:T], mean_w[:, :], o_sq[:, m, :], start=(m == 0), stop=(m == VT - 1))
                step(mm)

            def rwkv(p):
                def step(mm):
                    mm.then_inc(rw_pe, 1)

                def after(s, steps, name):
                    pe.wait_ge(s, at(steps, name, p))
                pe.wait_ge(rw_dve, p * len(RW_DVE))
                pe.wait_ge(pp_landed, p * 32 + 32)
                pe.matmul(psum[:, 4, 0:T], pp[0:64, 0:P], lora[0:64, 0, :], start=True, stop=True)
                pe.matmul(psum[:, 5, 0:T], pp[64:P, 0:P], lora[64:P, 0, :], start=True, stop=True)
                pe.matmul(psum[:, 6, 0:T], pp[:, P:2 * P], lora[:, 1, :], start=True, stop=False)
                step(pe.matmul(psum[:, 6, 0:T], pp[0:GATE1, 2 * P:3 * P], lora[0:GATE1, 2, :], start=False, stop=True))
                after(rw_act, RW_ACT, "square")
                step(pe.matmul(psum[:, 7, 0:T], head_w[:, :], ksq[:, :], start=True, stop=True))
                after(rw_dve, RW_DVE, "abk")
                src = [ar[:, 0], bc[:, :], kc[:, :], rkv[:, 2]]
                for tt in range(2):
                    for n, s in enumerate(src):
                        transpose(psum[:, 4 + tt, n * P:(n + 1) * P], s[:, tt * P:(tt + 1) * P])
                for n, s in enumerate(src):
                    mm = transpose(psum[0:NS, 6, n * P:(n + 1) * P], s[:, SEQ:T])
                step(mm)
                after(rw_dve, RW_DVE, "rk")
                step(pe.matmul(psum[:, 7, 0:T], head_w[:, :], rk[:, :], start=True, stop=True))
                after(rw_act, RW_ACT, "turned_out")
                for n, s in enumerate((bc, kc)):
                    if n:
                        after(rw_dve, RW_DVE, "bonus")
                    for hd in range(2):
                        r = slice(64 * hd, 64 * hd + 64)
                        for tt in range(2):
                            cols = slice(tt * P, (tt + 1) * P)
                            mm = pe.matmul(psum[:, 4 + 2 * n + hd, tt * 256:tt * 256 + 256], s[r, cols], ar[r, :, cols],
                                           start=True, stop=True, skip_group_check=True)
                    step(mm)
                after(rw_dve, RW_DVE, "masked_b")
                pe.sem_inc(parted, 1)
                for hd in range(2):
                    r = slice(64 * hd, 64 * hd + 64)
                    for n, s in enumerate((bc, kc)):
                        c = n * 2 * NS
                        mm = pe.matmul(psum[0:NS, 4 + hd, c:c + 2 * NS], s[r, SEQ:T], ar[r, :, SEQ:T],
                                       start=True, stop=True, skip_group_check=True)
                step(mm)
                after(rw_dve, RW_DVE, "masked_s")
                after(rw_act, RW_ACT, "eye")
                after(rw_pool, RW_POOL, "lm1")
                ev = ident[:, :].rearrange("p (b two) -> p b two", two=2)[:, :, 0]
                for q in range(4):
                    mm = pe.matmul(psum[:, 5, q * 64:(q + 1) * 64], lm[:, q, :], ev, start=True, stop=True)
                for hd in range(2):
                    mm = pe.matmul(psum[0:NS, 5, 256 + hd * 16:272 + hd * 16], lm_s[:, hd, :], ev[0:NS, 0:16],
                                   start=True, stop=True)
                step(mm)
                before = "x1"
                for s in LEVELS:
                    after(rw_pool, RW_POOL, f"lm{s}")
                    after(rw_dve, RW_DVE, before)
                    for q in range(4):
                        mm = pe.matmul(psum[:, 5, q * P:(q + 1) * P], lm[:, q, :], xm[:, q, :], start=True, stop=True)
                    if s == 2:
                        for hd in range(2):
                            mm = pe.matmul(psum[0:NS, 4, hd * NS:(hd + 1) * NS], lm_s[:, hd, :], xm_s[:, hd, :],
                                           start=True, stop=True)
                    step(mm)
                    after(rw_act, RW_ACT, f"y_out{s}")
                    for q in range(4):
                        y1 = ym[:, q, :].rearrange("p (b two s) -> p b two s", two=2, s=s)[:, :, 0, :]
                        x2 = xt[:, q, :].rearrange("p (b two s) -> p b two s", two=2, s=s)[:, :, 1, :]
                        if s < 32:
                            pe.matmul(psum[:, 6, q * 64:(q + 1) * 64], xt[:, q, :], y1, start=True, stop=True)
                        mm = pe.matmul(psum[:, 7, q * 64:(q + 1) * 64], ym[:, q, :], x2, start=True, stop=True)
                    if s == 2:
                        for hd in range(2):
                            x2 = xt_s[:, hd, :].rearrange("p (b two s) -> p b two s", two=2, s=s)[:, :, 1, :]
                            mm = pe.matmul(psum[0:NS, 7, 256 + hd * 16:272 + hd * 16], ym_s[:, hd, :], x2,
                                           start=True, stop=True)
                    step(mm)
                    before = f"x{s}"
                after(rw_dve, RW_DVE, f"x{LEVELS[-1]}")
                for hd in range(2):
                    v = slice(64 * hd, 64 * hd + 64)
                    for tt in range(2):
                        pe.matmul(psum[:, 4, tt * P + hd * 64:tt * P + hd * 64 + 64], nt[:, 2 * hd + tt, :],
                                  tok[:, tt, 3, v], start=True, stop=True)
                    mm = pe.matmul(psum[0:NS, 4, 256 + hd * 64:320 + hd * 64], ms[:, 2 * hd + 1, 0, :], tok_s[:, 3, v],
                                   start=True, stop=True)
                step(mm)
                after(rw_act, RW_ACT, "nv_out")
                for hd in range(2):
                    v = slice(64 * hd, 64 * hd + 64)
                    for tt in range(2):
                        pe.matmul(psum[:, 5, tt * P + hd * 64:tt * P + hd * 64 + 64], xt[:, 2 * hd + tt, :], nv[:, tt, v],
                                  start=True, stop=True)
                        pe.matmul(psum[v, 6, tt * P:(tt + 1) * P], tok[:, tt, 0, v], xt[:, 2 * hd + tt, :],
                                  start=True, stop=True)
                    pe.matmul(psum[0:NS, 5, 256 + hd * 64:320 + hd * 64], xt_s[:, hd, :], nv[0:NS, 2, v],
                              start=True, stop=True)
                    mm = pe.matmul(psum[v, 6, 256:256 + NS], tok_s[:, 0, v], xt_s[:, hd, :], start=True, stop=True)
                step(mm)
                for c in range(4):
                    tt, off = divmod(c * CH, P)
                    r = slice(off, off + CH)
                    if c == 0:
                        after(rw_dve, RW_DVE, "g_out")
                        after(rw_act, RW_ACT, "h_out")
                    else:
                        after(rw_dve, RW_DVE, f"s{c}")
                        step(pe.matmul(psum[r, 4, 0:P], hT[:, tt, r], st[:, c - 1, :], start=True, stop=True))
                        after(rw_dve, RW_DVE, f"u{c}")
                    pe.matmul(psum[:, 7, 0:P], tok[r, tt, 1, :], um[r, tt, :], start=True, stop=False)
                    step(pe.matmul(psum[:, 7, 0:P], tok[r, tt, 2, :], tok[r, tt, 3, :], start=False, stop=True))
                for bb in range(SB):
                    for hd in range(2):
                        v = slice(64 * hd, 64 * hd + 64)
                        mm = pe.matmul(psum[v, 5, bb * 8:bb * 8 + 8], s0[v, bb, :], hr[v, :, bb * ST:(bb + 1) * ST],
                                       start=True, stop=True, skip_group_check=True)
                step(mm)
                after(rw_act, RW_ACT, "us_out")
                step(transpose(psum[0:NS, 6, 0:P], us[:, 0, :]))
                after(rw_dve, RW_DVE, "ub")
                for q in range(2):
                    bs = slice(4 * q, 4 * q + 4)
                    pe.matmul(psum[:, 4 + q, :], tok_s[:, 1, :], ub[:, bs, :], start=True, stop=False)
                    mm = pe.matmul(psum[:, 4 + q, :], tok_s[:, 2, :], vb[:, bs, :], start=False, stop=True)
                step(mm)
                after(rw_dve, RW_DVE, "s4")
                for tt in range(2):
                    for hd in range(2):
                        v = slice(64 * hd, 64 * hd + 64)
                        pe.matmul(psum[v, 7, tt * P:(tt + 1) * P], tok[:, tt, 3, v], qt[:, 2 * hd + tt, :],
                                  start=(tt == 0), stop=False, skip_group_check=True)
                        pe.matmul(psum[v, 7, tt * P:(tt + 1) * P], um[:, tt, v], pt[:, 2 * hd + tt, :],
                                  start=False, stop=False, skip_group_check=True)
                for c in range(1, 4):
                    pe.matmul(psum[:, 7, c * CH:(c + 1) * CH], st[:, c - 1, :], ar[:, 1, c * CH:(c + 1) * CH],
                              start=False, stop=True, skip_group_check=True)
                for hd in range(2):
                    v = slice(64 * hd, 64 * hd + 64)
                    pe.matmul(psum[v, 7, SEQ:T], tok_s[:, 3, v], ms[:, 2 * hd + 1, 1, :], start=False, stop=False,
                              skip_group_check=True)
                    mm = pe.matmul(psum[v, 7, SEQ:T], um_s[:, v], ms[:, 2 * hd, 1, :], start=False, stop=True,
                                   skip_group_check=True)
                step(mm)
                after(rw_dve, RW_DVE, "y")
                step(pe.matmul(psum[:, 6, 0:T], head_w[:, :], ysb[:, :], start=True, stop=True))
                after(rw_act, RW_ACT, "y_square")
                step(pe.matmul(psum[:, 4, 0:T], head_w[:, :], ksq[:, :], start=True, stop=True))

            pe.wait_ge(lora_made, 1)
            pe.wait_ge(mix_loaded, 16 * MIX_LOADS)
            with pe.Fori(0, RH) as i:
                projections(i)
                retention(i)
                pe.wait_ge(ret_dve, at(RET_DVE, "done", i))
                for q in range(2):
                    rwkv(i * 2 + q)

            pe.wait_ge(o_lo, RH * VT + PAIRS)
            with pe.Fori(0, PAIRS) as i:
                pair(i, (*ret_o_ph, 4, 2), 0, 0, 2, KT, h_hi, h_lo)
                pair(i, (*ret_o_ph, 4, 2), 2, 1, 2, KT, or_hi, or_lo)
            with pe.Fori(0, PAIRS) as i:
                pair(i, (*rw_o_ph, 4, 2), 0, 0, 2, KT, h_hi, h_lo)
                pair(i, (*rw_o_ph, 4, 2), 2, 1, 2, PAIRS, ow_hi, ow_lo)
            pe.wait_ge(merged_lo, PAIRS)
            with pe.Fori(0, 4) as i:
                pair(i, (*w_out_ph, 4, 2), 0, 0, 2, KT, m_hi, m_lo)
                pair(i, (*w_out_ph, 4, 2), 2, 1, 2, KT, m_hi, m_lo)
            feed(1)
            norm(3)

        @block.scalar
        def _(act):
            ch = Chain(act, act_chain)

            def split(n, first, cols=BLK):
                slot = first % 2
                act.wait_ge(raw_landed[slot], n * 8 + 16 * (first // 2 + 1))
                wait(act, used, n + (first - 1))
                act.activation(w_hi[:, slot, 0:cols], raw[:, slot, 0:cols], ACT.Copy).then_inc(hi_made, 1)

            def norm(r):
                for k in range(KT):
                    if k % 2 == 0:
                        act.wait_ge(x_made, r * (KT // 2) + k // 2 + 1)
                    wait(act, square_used, r * KT + k - 1)
                    act.activation(sq[:, k % 2, :], x[:, k, :], ACT.Square).then_inc(squares, 1)
                act.wait_ge(square_used, (r + 1) * KT)
                act.activation(scale[:, :], psum[:, 4, 0:T], ACT.Sqrt, bias=eps_c[:, 0:1]).then_inc(root_made, 1)
                if r < 3:
                    for k in range(KT):
                        act.wait_ge(normed, r * KT + k + 1)
                        act.activation(h_hi[:, k, :], prod[:, k % 2, :], ACT.Copy).then_inc(normed_hi, 1)

            act.wait_ge(loaded, 16 * LOADS)

            def feed(n):
                norm(2 * n)
                for f in range(2):
                    (b, g), (bd, _) = ffn[n][f]
                    done = (2 * n + f) * (HT // 2)
                    gates = done + n * 2 * PAIRS

                    def hidden_part(i):
                        act.wait_ge(hidden, i + (done + 1))
                        act.activation(g_hi[:, bass.ds(i * 2, 2), :], prod[:, :, :], ACT.Copy).then_inc(hidden_hi, 1)

                    def up(i):
                        split(i * 4, b)
                        split(i * 4, b + 1)
                        if not is_first(i):
                            hidden_part(i - 1)
                        split(i * 4, b + 2)
                        split(i * 4, b + 3)
                        act.wait_ge(used, i * 4 + (b + 2))
                        wait(act, hidden, i + done)
                        act.activation(gate[:, :, :], psum[:, 2 * (g % 2):2 * (g % 2) + 2, 0:T],
                                       ACT.Silu).then_inc(gate_made, 1)
                        act.wait_ge(gate_made, i + (gates + 1))
                        act.sem_inc(psum_free[g % 2], 1)
                    loop(act, HT // 2, up)
                    hidden_part(HT // 2 - 1)

                    def down(i):
                        for j in range(8):
                            split(i * 8, bd + j, DOWN)
                    loop(act, 4, down)

            feed(0)
            norm(1)
            b, g = lora_ph
            split(0, b)
            split(0, b + 1)
            split(0, b + 2, LORA2)

            def z_copy(dst, tiles, g, w=P):
                s = 2 * (g % 2)
                ch.do(act.activation(dst[0:w, 0:tiles, 1:1 + SEQ], psum[0:w, s:s + tiles, 0:SEQ], ACT.Copy), wait=False)
                sample = dst[0:w, 0:tiles, 1 + SEQ:].rearrange("p a (b t) -> p a b t", t=ST + 1)
                for a in range(tiles):
                    ins = act.activation(sample[:, a, :, 1:], psum[0:w, s + a, SEQ:T].rearrange("p (b t) -> p b t", t=ST),
                                         ACT.Copy)
                    if a < tiles - 1:
                        ch.do(ins, wait=False)
                ins.then_inc(psum_free[g % 2], 1)

            act.wait_ge(spilled, 16)
            act.wait_ge(used, b + 2)
            z_copy(zs[:, 0], 2, g)
            act.wait_ge(used, b + 3)
            z_copy(zs[:, 1], 1, g + 1, GATE1)
            act.wait_ge(lora_shifted, 1)
            ch.do(act.activation(lora[0:64, 0, :], rkv[0:64, 0, :], ACT.Tanh), wait=False)
            ch.do(act.activation(lora[64:P, 0, :], rkv[64:P, 0, :], ACT.Copy), wait=False)
            ch.do(act.activation(lora[:, 1, :], rkv[:, 1, :], ACT.Sigmoid), wait=False)
            act.activation(lora[0:GATE1, 2, :], rkv[0:GATE1, 2, :], ACT.Sigmoid).then_inc(lora_made, 1)
            act.wait_ge(lora_made, 1)

            def projections(i):
                b, g = mix_ph

                def read_out(j):
                    act.wait_ge(used, i * 18 + (b + (2 * j + 2 if j < 8 else 9 + j)))
                    s = 2 * ((g + j) % 2)
                    if j < 3:
                        return z_copy(zs[:, j], 2, g + j)
                    elif j < 7:
                        ins = act.activation(vg[:, 0, 2 * (j - 5):2 * (j - 5) + 2, :], psum[:, s:s + 2, 0:T], ACT.Copy)
                    elif j == 7:
                        ins = act.activation(vg[:, 1, 0:2, :], psum[:, s:s + 2, 0:T], ACT.Silu)
                    else:
                        ins = act.activation(vg[:, 1, j - 6, :], psum[:, s, 0:T], ACT.Silu)
                    ins.then_inc(psum_free[(g + j) % 2], 1)
                n = 0
                for j in range(10):
                    split(i * 18, b + n)
                    n += 1
                    if j and j - 1 not in (3, 4):
                        read_out(j - 1)
                    if j < 8:
                        split(i * 18, b + n)
                        n += 1
                read_out(9)

            def retention(h):
                def step(ins):
                    ins.then_inc(ret_act, 1)

                def after(s, steps, name):
                    act.wait_ge(s, at(steps, name, h))
                mixed_in(act, h)
                after(ret_pe, RET_PE, "v_turned")
                ch.do(act.activation(v_tok[:, :, :], psum[:, 4:6, :], ACT.Copy), wait=False)
                step(act.activation(v_tok_s[:, :], psum[0:NS, 6, :], ACT.Copy))
                after(ret_pe, RET_PE, "k_turned")
                act.wait_ge(rc_landed, h * 16 + 16)
                act.wait_ge(rp_sent, h * 32)
                for tt in range(2):
                    ch.do(act.activation(k_tok[:, tt, :], psum[:, 7, tt * 256:(tt + 1) * 256], ACT.Copy,
                                         scale=rc[:, 448 + tt:449 + tt]), wait=False)
                step(act.activation(k_tok_s[:, :], psum[0:NS, 6, 0:256], ACT.Copy, scale=rc[0:NS, 450:451]))
                for e in range(2):
                    after(ret_pe, RET_PE, f"kv{e}")
                    step(act.activation(s_out[:, e, :], psum[:, 6 + e, :], ACT.Copy))
                after(ret_pe, RET_PE, "o_prompt")
                step(act.activation(o_T[:, :, 0:SEQ], psum[:, 4:6, :].rearrange("p b (m t) -> p (b m) t", m=2), ACT.Copy))
                after(ret_dve, RET_DVE, "o_sample_out")
                after(ret_act, RET_ACT, "o_prompt_out")
                step(act.activation(o_sq[:, :, :], o_T[:, :, :], ACT.Square))
                after(ret_pe, RET_PE, "norm")
                step(act.activation(r_scale[:, :], psum[:, 7, 0:T], ACT.Sqrt, bias=eps_c[:, 0:1], scale=float(D // DV)))

            def rwkv(p):
                def step(ins):
                    ins.then_inc(rw_act, 1)

                def after(s, steps, name):
                    act.wait_ge(s, at(steps, name, p))
                c = lambda n: pp[:, n:n + 1]
                after(rw_pe, RW_PE, "lora")
                ch.do(act.activation(wag[:, 0, :], psum[:, 4, 0:T], ACT.Sigmoid, bias=c(C_W0)), wait=False)
                ch.do(act.activation(wag[:, 1, :], psum[:, 5, 0:T], ACT.Sigmoid, bias=c(C_A0)), wait=False)
                step(act.activation(wag[:, 2, :], psum[:, 6, 0:T], ACT.Copy))
                after(rw_dve, RW_DVE, "shifted")
                step(act.activation(ksq[:, :], rkv[:, 1, :], ACT.Square, scale=c(C_KK)))
                after(rw_dve, RW_DVE, "kk_max")
                step(act.activation(kn[:, :], kn[:, :], ACT.Sqrt))
                after(rw_dve, RW_DVE, "summed")
                ch.do(act.activation(decays[:, 0, :], csum[:, 0, :], ACT.Exp, scale=-KAPPA), wait=False)
                ch.do(act.activation(decays[:, 1, :], csum[:, 0, :], ACT.Exp, scale=KAPPA), wait=False)
                step(act.activation(decays[:, 2, :], csum[:, 1, :], ACT.Exp, scale=-KAPPA))
                after(rw_pe, RW_PE, "turned")
                ch.do(act.activation(tok[:, :, :, :].rearrange("p a b c -> p a (b c)"), psum[:, 4:6, :], ACT.Copy), wait=False)
                step(act.activation(tok_s[:, :, :].rearrange("p b c -> p (b c)"), psum[0:NS, 6, :], ACT.Copy))
                ch.do(act.activation(xm[:, :, :], ident[:, :].unsqueeze(1).broadcast_to([P, 4, P]), ACT.Copy), wait=False)
                step(act.activation(xm_s[:, :, :], ident[0:NS, 0:NS].unsqueeze(1).broadcast_to([NS, 2, NS]), ACT.Copy))
                for s in LEVELS:
                    after(rw_pe, RW_PE, f"y{s}")
                    if s == 2:
                        ch.do(act.activation(ym_s[:, :, :].rearrange("p a b -> p (a b)"), psum[0:NS, 4, 0:2 * NS], ACT.Copy), wait=False)
                    step(act.activation(ym[:, :, :].rearrange("p a b -> p (a b)"), psum[:, 5, :], ACT.Copy))
                after(rw_pe, RW_PE, "nv")
                ch.do(act.activation(nv[:, 0:2, :].rearrange("p a b -> p (a b)"), psum[:, 4, 0:256], ACT.Copy), wait=False)
                step(act.activation(nv[0:NS, 2, :], psum[0:NS, 4, 256:384], ACT.Copy))
                after(rw_pe, RW_PE, "gh")
                ch.do(act.activation(hT[:, :, :].rearrange("p a b -> p (a b)"), psum[:, 6, 0:256], ACT.Copy), wait=False)
                ch.do(act.activation(hr[:, 1, :], ar[:, 1, SEQ:T], ACT.Copy), wait=False)
                step(act.activation(hr[:, 0, :], psum[:, 6, 256:256 + NS], ACT.Copy))
                after(rw_pe, RW_PE, "u_s")
                step(act.activation(us[:, :, :].rearrange("p a (b t) -> p b a t", t=ST),
                                    psum[:, 5, 0:64].rearrange("p (b a t) -> p b a t", a=2, t=ST), ACT.Copy))
                after(rw_pe, RW_PE, "out")
                step(act.activation(ysb[:, 0:SEQ], psum[:, 7, 0:SEQ], ACT.Copy))
                after(rw_dve, RW_DVE, "centred")
                step(act.activation(ksq[:, :], yc[:, :], ACT.Square))
                after(rw_pe, RW_PE, "var")
                step(act.activation(kn[:, :], psum[:, 4, 0:T], ACT.Sqrt, bias=eps_c[:, 1:2]))

            def mix_step(i):
                projections(i)
                retention(i)
                act.wait_ge(ret_dve, at(RET_DVE, "done", i))
                for q in range(2):
                    rwkv(i * 2 + q)
                    act.wait_ge(rw_dve, at(RW_DVE, "done", i * 2 + q))
            ch.loop(RH, mix_step)

            mixing_over(act)
            for k in range(RH * VT):
                act.activation(or_hi[:, k, :], o_ret[:, k, :], ACT.Copy).then_inc(o_hi, 1)
            act.wait_ge(o_lo, RH * VT)
            for k in range(PAIRS):
                act.activation(ow_hi[:, k, :], o_rw[:, k, :], ACT.Copy).then_inc(o_hi, 1)

            def merge(n, ph, cols):
                b, g = ph

                def hi_part(i):
                    act.wait_ge(merged, i + 1)
                    act.activation(m_hi[:, bass.ds(i * 2, 2), :], prod_m[:, :, :], ACT.Copy).then_inc(merged_hi, 1)

                def body(i):
                    split(i * 4, b)
                    split(i * 4, b + 1)
                    if n and not is_first(i):
                        hi_part(i - 1)
                    for j in range(2, 4):
                        split(i * 4, b + j, cols)
                    act.wait_ge(used, i * 4 + (b + 2))
                    wait(act, gate_used, i + n * PAIRS)
                    act.activation(gate_m[:, :, :], psum[:, 2 * (g % 2):2 * (g % 2) + 2, 0:T],
                                   ACT.Sigmoid).then_inc(gate_made, 1)
                    act.wait_ge(gate_made, i + (2 * (HT // 2) + n * PAIRS + 1))
                    act.sem_inc(psum_free[g % 2], 1)
                loop(act, PAIRS, body)
                if n:
                    hi_part(PAIRS - 1)
            merge(0, ret_o_ph, BLK)
            merge(1, rw_o_ph, BLK // 2)

            def out(i):
                for j in range(4):
                    split(i * 4, w_out_ph[0] + j)
            loop(act, 4, out)
            feed(1)
            norm(3)

        @block.vector
        def _(dve):
            ch = Chain(dve, dve_chain)
            do = ch.do

            def split(n, first, cols=BLK):
                slot = first % 2
                dve.wait_ge(hi_made, n + (first + 1))
                dve.tensor_tensor(w_lo[:, slot, 0:cols], raw[:, slot, 0:cols], w_hi[:, slot, 0:cols].bitcast(F32),
                                  ALU.subtract).then_inc(lo_made, 1)

            def norm(r):
                dve.wait_ge(root_made, r + 1)
                do(dve.reciprocal(scale[:, :], scale[:, :]))

                def tile(k):
                    out = x[:, k, :] if r == 3 else prod[:, k % 2, :]
                    dve.scalar_tensor_tensor(out=out, in0=x[:, k, :], scalar=gains[:, r, k:k + 1], in1=scale[:, :],
                                             op0=ALU.mult, op1=ALU.mult).then_inc(normed, 1)
                tile(0)
                for k in range(KT):
                    if k + 1 < KT:
                        if k >= 1 and r < 3:
                            dve.wait_ge(normed_lo, r * KT + k)
                        tile(k + 1)
                    if r < 3:
                        dve.wait_ge(normed_hi, r * KT + k + 1)
                        dve.tensor_tensor(h_lo[:, k, :], prod[:, k % 2, :], h_hi[:, k, :].bitcast(F32),
                                          ALU.subtract).then_inc(normed_lo, 1)

            dve.wait_ge(loaded, 16 * LOADS)
            do(dve.memset(eps_c[:, 0:1], EPS), wait=False)
            do(dve.memset(eps_c[:, 1:2], GN_EPS))
            dve.sem_inc(x_made, KT // 2)

            def feed(n):
                norm(2 * n)
                for f in range(2):
                    (b, g), (bd, gd) = ffn[n][f]
                    done = (2 * n + f) * (HT // 2)
                    gates = done + n * 2 * PAIRS

                    def product(i):
                        dve.wait_ge(used, i * 4 + (b + 4))
                        dve.wait_ge(gate_made, i + (gates + 1))
                        wait(dve, hidden_lo, i + done)
                        s = 2 * ((g + 1) % 2)
                        dve.tensor_tensor(prod[:, :, :], psum[:, s:s + 2, 0:T], gate[:, :, :], ALU.mult).then_inc(hidden, 1)
                        dve.wait_ge(hidden, i + (done + 1))
                        dve.sem_inc(psum_free[(g + 1) % 2], 1)

                    def low(i):
                        dve.wait_ge(hidden_hi, i + (done + 1))
                        pr = bass.ds(i * 2, 2)
                        dve.tensor_tensor(g_lo[:, pr, :], prod[:, :, :], g_hi[:, pr, :].bitcast(F32),
                                          ALU.subtract).then_inc(hidden_lo, 1)

                    def up(i):
                        split(i * 4, b)
                        if not is_first(i):
                            product(i - 1)
                        split(i * 4, b + 1)
                        if not is_first(i):
                            low(i - 1)
                        split(i * 4, b + 2)
                        split(i * 4, b + 3)
                    loop(dve, HT // 2, up)
                    product(HT // 2 - 1)
                    low(HT // 2 - 1)
                    add(4, 8, bd, gd, DOWN, 0.5, f == 1)

            def add(times, per, b, g, cols, factor, final):
                def take(i, j):
                    dve.wait_ge(used, i * per + (b + (j + 1) * per // 2))
                    s = 2 * ((g + j) % 2)
                    pr = bass.ds(i * 4 + 2 * j, 2)
                    do(dve.scalar_tensor_tensor(out=x[:, pr, :], in0=psum[:, s:s + 2, 0:T], scalar=factor, in1=x[:, pr, :],
                                                op0=ALU.mult, op1=ALU.add))
                    dve.sem_inc(psum_free[(g + j) % 2], 1)
                    if final:
                        dve.sem_inc(x_made, 1)

                def body(i, tail=True):
                    for j in range(per):
                        split(i * per, b + j, cols)
                        if j == per // 2:
                            take(i, 0)
                    take(i, 1)
                ch.loop(times, body)

            feed(0)
            norm(1)
            b, g = lora_ph
            split(0, b)
            split(0, b + 1)
            split(0, b + 2, LORA2)
            dve.wait_ge(spilled, 16)
            dve.wait_ge(mix_loaded, 16 * MIX_LOADS)
            do(dve.memset(zs[:, :, :, 0:1], 0.0), wait=False)
            do(dve.memset(last[:, :, :], 0.0), wait=False)
            def samples(v):
                return v.rearrange("p (b t) -> p b t", t=ST + 1)

            def shift(out, tmp, z, mu):
                do(dve.tensor_tensor(tmp[:, 0:SEQ], z[:, 0:SEQ], z[:, 1:1 + SEQ], ALU.subtract), wait=False)
                zq = samples(z[:, 1 + SEQ:])
                tq, oq = (v[:, SEQ:T].rearrange("p (b t) -> p b t", t=ST) for v in (tmp, out))
                do(dve.tensor_tensor(tq, zq[:, :, 0:ST], zq[:, :, 1:], ALU.subtract))
                do(dve.scalar_tensor_tensor(out=out[:, 0:SEQ], in0=tmp[:, 0:SEQ], scalar=mu, in1=z[:, 1:1 + SEQ],
                                            op0=ALU.mult, op1=ALU.add), wait=False)
                do(dve.scalar_tensor_tensor(out=oq, in0=tq, scalar=mu, in1=zq[:, :, 1:], op0=ALU.mult, op1=ALU.add))

            for s in range(2):
                dve.wait_ge(psum_free[s], g // 2 + 1)
            for k in range(3):
                w = P if k < 2 else GATE1
                z = zs[0:w, k // 2, k % 2, :]
                do(dve.tensor_copy(samples(z[:, 1 + SEQ:])[:, :, 0], lpk[0:w, k * SB:(k + 1) * SB]))
                shift(rkv[0:w, k, :], shifted[0:w, k, :], z, lpk[0:w, 3 * SB + k:3 * SB + k + 1])
                do(dve.tensor_copy(last[0:w, k, 0:1], z[:, SEQ:SEQ + 1]), wait=False)
                do(dve.tensor_copy(last[0:w, k, 1:], samples(z[:, 1 + SEQ:])[:, :, ST]))
            dve.sem_inc(lora_shifted, 1)
            dve.sem_inc(last_made, 1)

            def projections(i):
                b, g = mix_ph

                def rotate(j):
                    dve.wait_ge(used, i * 18 + (b + 2 * j + 2))
                    s = 2 * ((g + j) % 2)
                    factor = 1.0 if j == 3 else DK ** -0.5

                    def times(n, bank, t):
                        do(dve.scalar_tensor_tensor(out=rot[:, n, :], in0=psum[:, bank, 0:T], scalar=factor,
                                                    in1=trig[:, t, :], op0=ALU.mult, op1=ALU.mult), wait=(n == 1))
                    times(0, s, 0)
                    times(1, s + 1, 1)
                    do(dve.tensor_tensor(qk[:, 2 * (j - 3), :], rot[:, 0, :], rot[:, 1, :], ALU.subtract))
                    times(0, s, 1)
                    times(1, s + 1, 0)
                    dve.sem_inc(psum_free[(g + j) % 2], 1)
                    do(dve.tensor_tensor(qk[:, 2 * (j - 3) + 1, :], rot[:, 0, :], rot[:, 1, :], ALU.add))
                n = 0
                for j in range(10):
                    split(i * 18, b + n)
                    n += 1
                    if j - 1 in (3, 4):
                        rotate(j - 1)
                    if j < 8:
                        split(i * 18, b + n)
                        n += 1
                mixed_in(dve, i)
                dve.wait_ge(last_sent, i * 16 + 16)
                for a in range(3):
                    for q in range(2):
                        z = zs[:, a, q, :]
                        do(dve.tensor_copy(last[:, 2 * a + q, 0:1], z[:, SEQ:SEQ + 1]), wait=False)
                        do(dve.tensor_copy(last[:, 2 * a + q, 1:], samples(z[:, 1 + SEQ:])[:, :, ST]), wait=(a + q == 3))
                dve.sem_inc(last_made, 1)

            def retention(h):
                def after(s, steps, name):
                    dve.wait_ge(s, at(steps, name, h))

                def step(ins):
                    ins.then_inc(ret_dve, 1)
                dve.wait_ge(rc_landed, h * 16 + 16)
                do(dve.tensor_tensor(q_s[:, 0, :], qk[:, 0, SEQ:T], rc[:, 416:448], ALU.mult), wait=False)
                step(dve.tensor_tensor(q_s[:, 1, :], qk[:, 1, SEQ:T], rc[:, 416:448], ALU.mult))
                after(ret_pe, RET_PE, "scores")
                do(dve.tensor_tensor(scores[:, 0:SEQ], psum[:, 4, 0:SEQ], rc[:, 0:SEQ], ALU.mult), wait=False)
                do(dve.tensor_tensor(scores[:, SEQ:384], psum[:, 5, 0:P], rc[:, 0:P], ALU.mult), wait=False)
                step(dve.tensor_tensor(scores[0:NS, 384:384 + NS], psum[0:NS, 5, P:P + NS], rc[0:NS, 384:384 + NS], ALU.mult))
                after(ret_act, RET_ACT, "k_out")
                step(dve.tensor_tensor(k_own[:, :, :], k_tok_s[:, :].unsqueeze(1).broadcast_to([NS, SB, DK]),
                                       own[:, :].unsqueeze(2).broadcast_to([NS, SB, DK]), ALU.mult))
                for bb in range(SB):
                    for n, e in enumerate("eo"):
                        after(ret_pe, RET_PE, f"kv_s{bb}{e}")
                        bank = (7, 4, 5)[(2 * bb + n) % 3]
                        dve.scalar_tensor_tensor(out=s_ret[:, bb % SLOTS, n, :], in0=s_ret[:, bb % SLOTS, n, :],
                                                 scalar=rc[:, 451:452], in1=psum[:, bank, :], op0=ALU.mult,
                                                 op1=ALU.add).then_inc(s_new, 1)
                step(dve.tensor_copy(o_T[:, :, SEQ:T], psum[:, 6, 0:VT * NS].rearrange("p (m t) -> p m t", m=VT)))
                after(ret_act, RET_ACT, "root")
                do(dve.reciprocal(r_scale[:, :], r_scale[:, :]), wait=False)
                do(dve.tensor_tensor(o_T[:, :, :], o_T[:, :, :], vg[:, 1, :, :], ALU.mult))
                step(dve.tensor_tensor(o_ret[:, bass.ds(h * VT, VT), :], o_T[:, :, :],
                                       r_scale[:, :].unsqueeze(1).broadcast_to([P, VT, T]), ALU.mult))
                after(ret_dve, RET_DVE, "done")

            def rwkv(p, q):
                def after(s, steps, name):
                    dve.wait_ge(s, at(steps, name, p))

                def step(ins):
                    ins.then_inc(rw_dve, 1)

                def c(n):
                    return pp[:, n:n + 1]

                def mul(out, a, b, wait=True):
                    do(dve.tensor_tensor(out, a, b, ALU.mult), wait=wait)
                r_, k_, v_ = (rkv[:, n, :] for n in range(3))
                dve.wait_ge(pp_landed, p * 32 + 32)
                do(dve.tensor_scalar(c(C_OKA), c(C_KA), -1.0, 1.0, ALU.mult, ALU.add), wait=False)
                for a in range(3):
                    z = zs[:, a, q, :]
                    do(dve.tensor_copy(samples(z[:, 1 + SEQ:])[:, :, 0], pp[:, C_SHIFT + a * SB:C_SHIFT + (a + 1) * SB]))
                    shift(rkv[:, a, :], shifted[:, a, :], z, c(C_MU + a))
                dve.sem_inc(rw_dve, 1)
                after(rw_act, RW_ACT, "gates")
                do(dve.tensor_tensor_scan(csum[:, 0, :], run_m[:, :], wag[:, 0, :], 0.0, ALU.mult, ALU.add))
                step(dve.tensor_tensor(csum[:, 1, :], csum[:, 0, :], wag[:, 0, :], ALU.subtract))
                after(rw_pe, RW_PE, "kk_sum")
                step(dve.tensor_scalar(kn[:, :], psum[:, 7, 0:T], float(N), 1e-24, ALU.mult, ALU.max))
                do(dve.tensor_scalar(rk[:, :], wag[:, 1, :], c(C_KA), c(C_OKA), ALU.mult, ALU.add))
                mul(k2[:, :], k_, rk[:, :], wait=False)
                after(rw_act, RW_ACT, "root")
                do(dve.reciprocal(kn[:, :], kn[:, :]))
                do(dve.scalar_tensor_tensor(out=kk[:, :], in0=k_, scalar=c(C_KK), in1=kn[:, :], op0=ALU.mult, op1=ALU.mult))
                after(rw_act, RW_ACT, "exps")
                do(dve.scalar_tensor_tensor(out=ar[:, 0, :], in0=kk[:, :], scalar=-1.0, in1=decays[:, 2, :],
                                            op0=ALU.mult, op1=ALU.mult), wait=False)
                mul(ar[:, 1, :], r_, decays[:, 0, :], wait=False)
                mul(bc[:, :], kk[:, :], wag[:, 1, :])
                mul(kc[:, :], k2[:, :], decays[:, 1, :], wait=False)
                step(dve.tensor_tensor(bc[:, :], bc[:, :], decays[:, 1, :], ALU.mult))
                step(dve.scalar_tensor_tensor(out=rk[:, :], in0=k2[:, :], scalar=c(C_RK), in1=r_, op0=ALU.mult, op1=ALU.mult))
                after(rw_pe, RW_PE, "bonus")
                step(dve.scalar_tensor_tensor(out=bonus[:, :], in0=psum[:, 7, 0:T], scalar=float(N), in1=v_,
                                              op0=ALU.mult, op1=ALU.mult))
                for n, (name, x1, x2) in enumerate((("b", mt, pt), ("k", nt, qt))):
                    after(rw_pe, RW_PE, f"prod_{name}")
                    for hd in range(2):
                        src = psum[:, 4 + 2 * n + hd, :].rearrange("p (t a i) -> p t a i", t=2, a=2)
                        for a, dst in enumerate((x1, x2)):
                            ins = dve.tensor_tensor(dst[:, 2 * hd:2 * hd + 2, :], src[:, :, a, :],
                                                    tri[:, a, :].unsqueeze(1).broadcast_to([P, 2, P]), ALU.mult)
                            if hd == 1 and a == 1:
                                step(ins)
                            else:
                                do(ins, wait=False)
                after(rw_pe, RW_PE, "prod_s")
                tri2 = tri_s[:, :, :].rearrange("p a i -> p (a i)").unsqueeze(1).broadcast_to([NS, 2, 2 * NS])
                for hd in range(2):
                    ins = dve.tensor_tensor(ms[:, 2 * hd:2 * hd + 2, :, :].rearrange("p a b i -> p a (b i)"),
                                            psum[0:NS, 4 + hd, 0:4 * NS].rearrange("p (a b) -> p a b", a=2), tri2, ALU.mult)
                    step(ins) if hd else do(ins, wait=False)
                after(rw_pool, RW_POOL, "lm1")
                do(dve.tensor_tensor(xt[:, :, :], lm[:, :, :], ident[:, :].unsqueeze(1).broadcast_to([P, 4, P]), ALU.add), wait=False)
                do(dve.tensor_tensor(xt_s[:, :, :], lm_s[:, :, :], ident[0:NS, 0:NS].unsqueeze(1).broadcast_to([NS, 2, NS]),
                                     ALU.add), wait=False)
                after(rw_pe, RW_PE, "x1")
                ev = xm_s[:, :, :].rearrange("p q (b two) -> p q b two", two=2)[:, :, :, 0]
                do(dve.tensor_tensor(ev, ev, psum[0:NS, 5, 256:288].rearrange("p (q b) -> p q b", q=2), ALU.add), wait=False)
                ev = xm[:, :, :].rearrange("p q (b two) -> p q b two", two=2)[:, :, :, 0]
                step(dve.tensor_tensor(ev, ev, psum[:, 5, 0:256].rearrange("p (q b) -> p q b", q=4), ALU.add))
                for s in LEVELS:
                    after(rw_pe, RW_PE, f"d{s}")
                    if s == 2:
                        x2 = xt_s[:, :, :].rearrange("p q (b two s) -> p q b two s", two=2, s=s)
                        for hd in range(2):
                            do(dve.tensor_tensor(x2[:, hd, :, 1], x2[:, hd, :, 1],
                                                 psum[0:NS, 7, 256 + 16 * hd:272 + 16 * hd].rearrange("p (b s) -> p b s", s=s),
                                                 ALU.add), wait=False)
                    if s < 32:
                        x2 = xm[:, :, :].rearrange("p q (b two s) -> p q b two s", two=2, s=s)[:, :, :, 0]
                        do(dve.tensor_tensor(x2, x2, psum[:, 6, 0:256].rearrange("p (q b s) -> p q b s", q=4, s=s), ALU.add),
                           wait=False)
                    x2 = xt[:, :, :].rearrange("p q (b two s) -> p q b two s", two=2, s=s)[:, :, :, 1]
                    step(dve.tensor_tensor(x2, x2, psum[:, 7, 0:256].rearrange("p (q b s) -> p q b s", q=4, s=s), ALU.add))
                    after(rw_dve, RW_DVE, f"x{s}")
                after(rw_pe, RW_PE, "gh")
                do(dve.tensor_copy(gm[0:NS, 2, :], psum[0:NS, 5, 256:384]), wait=False)
                do(dve.tensor_copy(um[0:CH, 0, :], psum[0:CH, 5, 0:P]), wait=False)
                step(dve.tensor_copy(gm[:, 0:2, :].rearrange("p a b -> p (a b)"), psum[:, 5, 0:256]))
                for n in range(1, 5):
                    after(rw_pe, RW_PE, f"upd{n - 1}")
                    if n == 1:
                        do(dve.tensor_copy(stt[:, :], psum[:, 7, 0:P]))
                    else:
                        do(dve.tensor_tensor(stt[:, :], psum[:, 7, 0:P], st[:, n - 2, :], ALU.add))
                    step(dve.scalar_tensor_tensor(out=st[:, n - 1, :], in0=stt[:, :], scalar=decays[:, 0, n * CH - 1:n * CH],
                                                  in1=blocks_m[:, :], op0=ALU.mult, op1=ALU.mult))
                    after(rw_dve, RW_DVE, f"s{n}")
                    if n < 4:
                        tt, off = divmod(n * CH, P)
                        rr = slice(off, off + CH)
                        after(rw_pe, RW_PE, f"u{n}")
                        step(dve.tensor_tensor(um[rr, tt, :], psum[rr, 4, 0:P], gm[rr, tt, :], ALU.add))
                after(rw_pe, RW_PE, "u_s_turned")
                do(dve.tensor_tensor(um_s[:, :], psum[0:NS, 6, 0:P], gm[0:NS, 2, :], ALU.add), wait=False)
                own_b = own[:, :].unsqueeze(2).broadcast_to([NS, SB, P])
                mul(vb[:, :, :], tok_s[:, 3, :].unsqueeze(1).broadcast_to([NS, SB, P]), own_b)
                step(dve.tensor_tensor(ub[:, :, :], um_s[:, :].unsqueeze(1).broadcast_to([NS, SB, P]), own_b, ALU.mult))
                after(rw_pe, RW_PE, "upd_s")
                for hd in range(2):
                    v = slice(64 * hd, 64 * hd + 64)
                    do(dve.tensor_tensor(s0[v, :, :], s0[v, :, :],
                                         psum[v, 4:6, :].rearrange("p q (b c) -> p (q b) c", b=4)[:, :, v], ALU.add),
                       wait=(hd == 1))
                end = decays[:, 0, SEQ:T].rearrange("p (b t) -> p b t", t=ST)[:, :, ST - 1]
                step(dve.tensor_tensor(s0[:, :, :], s0[:, :, :], end.unsqueeze(2).broadcast_to([P, SB, N]), ALU.mult))
                after(rw_act, RW_ACT, "y_prompt_out")
                step(dve.tensor_tensor(ysb[:, SEQ:T], psum[:, 7, SEQ:T], us[:, 1, :], ALU.add))
                after(rw_pe, RW_PE, "mean")
                step(dve.tensor_tensor(yc[:, :], ysb[:, :], psum[:, 6, 0:T], ALU.subtract))
                after(rw_act, RW_ACT, "y_root")
                do(dve.reciprocal(kn[:, :], kn[:, :]))
                mul(yc[:, :], yc[:, :], kn[:, :])
                do(dve.tensor_scalar(yc[:, :], yc[:, :], c(C_LNW), c(C_LNB), ALU.mult, ALU.add))
                do(dve.tensor_tensor(yc[:, :], yc[:, :], bonus[:, :], ALU.add))
                step(dve.tensor_tensor(o_rw[:, bass.ds(p, 1), :].rearrange("p a t -> p (a t)"), yc[:, :], wag[:, 2, :], ALU.mult))
                after(rw_dve, RW_DVE, "done")

            def mix_step(i):
                projections(i)
                retention(i)
                units_free_of_retention(dve, i)
                for q in range(2):
                    rwkv(i * 2 + q, q)
                units_free_of_rwkv(dve, i)
            ch.loop(RH, mix_step)

            mixing_over(dve)
            for k in range(RH * VT):
                dve.wait_ge(o_hi, k + 1)
                dve.tensor_tensor(or_lo[:, k, :], o_ret[:, k, :], or_hi[:, k, :].bitcast(F32), ALU.subtract).then_inc(o_lo, 1)
            for k in range(PAIRS):
                dve.wait_ge(o_hi, RH * VT + k + 1)
                dve.tensor_tensor(ow_lo[:, k, :], o_rw[:, k, :], ow_hi[:, k, :].bitcast(F32), ALU.subtract).then_inc(o_lo, 1)

            def merge(n, ph, cols):
                b, g = ph
                s = 2 * ((g + 1) % 2)

                def product(i):
                    dve.wait_ge(used, i * 4 + (b + 4))
                    dve.wait_ge(gate_made, i + (2 * (HT // 2) + n * PAIRS + 1))
                    pr = bass.ds(i * 2, 2)
                    if n == 0:
                        do(dve.tensor_tensor(part[:, pr, :], psum[:, s:s + 2, 0:T], gate_m[:, :, :], ALU.mult))
                    else:
                        wait(dve, merged_lo, i)
                        do(dve.tensor_tensor(prod_m[:, :, :], psum[:, s:s + 2, 0:T], gate_m[:, :, :], ALU.mult))
                    dve.sem_inc(gate_used, 1)
                    dve.sem_inc(psum_free[(g + 1) % 2], 1)
                    if n:
                        dve.tensor_tensor(prod_m[:, :, :], prod_m[:, :, :], part[:, pr, :], ALU.add).then_inc(merged, 1)

                def low(i):
                    dve.wait_ge(merged_hi, i + 1)
                    pr = bass.ds(i * 2, 2)
                    dve.tensor_tensor(m_lo[:, pr, :], prod_m[:, :, :], m_hi[:, pr, :].bitcast(F32),
                                      ALU.subtract).then_inc(merged_lo, 1)

                def body(i):
                    split(i * 4, b)
                    split(i * 4, b + 1)
                    split(i * 4, b + 2, cols)
                    split(i * 4, b + 3, cols)
                    product(i)
                    if n:
                        low(i)
                ch.loop(PAIRS, body)
            merge(0, ret_o_ph, BLK)
            merge(1, rw_o_ph, BLK // 2)
            dve.wait_ge(x_back, 16)
            add(4, 4, *w_out_ph, BLK, 1.0, True)
            feed(1)
            norm(3)

        @block.gpsimd
        def _(pool):
            for dst, src in ((x, "x"), (mean_w, "mean_w"), (head_w, "head_w"), (ident, "ident"), (gains, "gains")):
                pool.dma_start(dst[:], d[src]).then_inc(loaded, 16)
            pool.wait_ge(normed_lo, 2 * KT)
            pool.dma_start(d["spill"], x[:, :, :]).then_inc(spilled, 16)
            pool.wait_ge(spilled, 16)
            for dst, src in ((trig, "trig"), (levels_m, "levels_m"), (tri, "tri"), (tri_s, "tri_s"), (own, "own"),
                             (blocks_m, "blocks_m"), (run_m, "run_m"), (lpk, "lpk")):
                pool.dma_start(dst[:], d[src]).then_inc(mix_loaded, 16)
            pool.wait_ge(last_made, 1)
            pool.dma_start(d["last_lora"], last[:, 0:3, :]).then_inc(last_sent, 16)
            pool.wait_ge(mix_loaded, 16 * MIX_LOADS)
            pool.wait_ge(lora_made, 1)

            def move(dst, src, done):
                pool.sem_inc(parted, 1)
                pool.dma_start(dst, src).then_inc(done, 16)

            def mix_step(i):
                units_free_of_rwkv(pool, i - 1) if not is_first(i) else None
                move(rc[:, :], d["rc"][i], rc_landed)
                per = 16 * (SB // SLOTS)

                def bring(bb):
                    s = bb % SLOTS
                    wait(pool, s_sent[s], i * per + 16 * (bb // SLOTS))
                    move(s_ret[:, s, :, :], d["s_ret"][i, bb], s_landed[s])
                for bb in range(SLOTS):
                    bring(bb)
                pool.wait_ge(last_made, i + 2)
                move(d["last"][i], last[:, :, :], last_sent)
                for e in range(2):
                    pool.wait_ge(ret_act, at(RET_ACT, f"state{e}", i))
                    move(d["ret_p"][i, e], s_out[:, e, :], rp_sent)
                for bb in range(SB):
                    pool.wait_ge(s_new, i * (2 * SB) + 2 * bb + 2)
                    move(d["ret_s"][i, bb], s_ret[:, bb % SLOTS, :, :], s_sent[bb % SLOTS])
                    if 1 <= bb <= SLOTS:
                        bring(bb - 1 + SLOTS)
                pool.wait_ge(ret_dve, at(RET_DVE, "done", i))
                units_free_of_retention(pool, i)
                for q in range(2):
                    p = i * 2 + q
                    if q:
                        pool.wait_ge(rw_dve, at(RW_DVE, "done", p - 1) if isinstance(p, int) else i * (2 * len(RW_DVE)) + len(RW_DVE))
                        pool.wait_ge(ws_sent, i * 32 + 16)
                        pool.wait_ge(wp_sent, i * 64 + 32)
                    move(pp[:, :], d["pp"][p], pp_landed)
                    move(s0[:, :, :], d["s0"][p], pp_landed)
                    for n, s in enumerate((1,) + LEVELS):
                        if s == 1:
                            pool.wait_ge(rw_dve, at(RW_DVE, "masked_s", p))
                        elif s == 2:
                            pool.wait_ge(rw_dve, at(RW_DVE, "x1", p))
                        else:
                            pool.wait_ge(rw_pe, at(RW_PE, f"y{s // 2}", p))
                        if s <= 2:
                            ins = pool.tensor_tensor(lm_s[:, :, :], ms[:, :, 0, :].rearrange("p (h n) i -> p h n i", n=2)[:, :, 0, :],
                                                     levels_m[0:NS, n, 0:NS].unsqueeze(1).broadcast_to([NS, 2, NS]), ALU.mult)
                        pool.tensor_tensor(lm[:, :, :], mt[:, :, :], levels_m[:, n, :].unsqueeze(1).broadcast_to([P, 4, P]),
                                           ALU.mult).then_inc(rw_pool, 1)
                    pool.wait_ge(rw_dve, at(RW_DVE, "s4", p))
                    for hd in range(2):
                        v = slice(64 * hd, 64 * hd + 64)
                        move(d["rwkv_p"][p, v, :], st[v, 3, v], wp_sent)
                    pool.wait_ge(rw_dve, at(RW_DVE, "s_s", p))
                    move(d["rwkv_s"][p], s0[:, :, :], ws_sent)
            loop(pool, RH, mix_step)
            mixing_over(pool)
            pool.wait_ge(used, w_out_ph[0])
            pool.dma_start(x[:, :, :], d["spill"]).then_inc(x_back, 16)


def consts():
    f = np.float32
    i = np.arange(P)
    j, i = np.meshgrid(i, i, indexing="ij")
    same = (j // CH == i // CH)
    tri = np.stack([same & (j < i), same & (j <= i)], 1)
    lev = np.stack([(j // (2 * s) == i // (2 * s)) & (j % (2 * s) < s) & (i % (2 * s) >= s)
                    for s in (1,) + LEVELS], 1)
    js, is_ = j[:NS, :NS], i[:NS, :NS]
    mine = js // ST == is_ // ST
    run = np.ones(T)
    run[:SEQ:CH] = 0
    run[SEQ::ST] = 0
    half = DK // 2
    inv = (f(1.0) / (f(10000.0) ** np.linspace(0.0, 1.0, half, dtype=f))).astype(f)
    pos = np.concatenate([np.arange(SEQ), 2048 + np.tile(np.arange(ST), SB)]).astype(f)
    ang = (inv[:, None] * pos[None, :]).astype(f)
    rc = np.zeros((RH, P, RC))
    for h in range(RH):
        lg = np.log(1.0 - 2.0 ** (-5.0 - h))
        row, col = np.arange(P)[:, None], np.arange(384)[None, :]
        rc[h, :, :384] = np.where(col >= row, np.exp(lg * np.maximum(col - row, 0)), 0)
        rc[h, :NS, 384:416] = np.where(mine & (js <= is_), np.exp(lg * np.maximum(is_ - js, 0)), 0)
        rc[h, :, 416:448] = np.exp(lg * (np.arange(NS) % ST + 1))
        rc[h, :, 448] = np.exp(lg * (SEQ - 1 - np.arange(P)))
        rc[h, :, 449] = np.exp(lg * (P - 1 - np.arange(P)))
        rc[h, :, 450] = np.exp(lg * (ST - 1 - np.arange(P) % ST))
        rc[h, :, 451] = np.exp(lg * ST)
    return {k: np.ascontiguousarray(v, dtype=f) for k, v in dict(
        mean_w=np.full((P, P), 1.0 / D), head_w=(j // N == i // N) / N, ident=np.eye(P),
        tri=tri, levels_m=lev, tri_s=np.stack([mine & (js < is_), mine & (js <= is_)], 1),
        own=np.arange(NS)[:, None] // ST == np.arange(SB)[None, :], blocks_m=(j // N == i // N),
        run_m=np.tile(run, (P, 1)), trig=np.stack([np.cos(ang), np.sin(ang)], 1), rc=rc).items()}


def kernel(**inputs):
    import concourse.bacc as bacc
    from concourse.bass_utils import run_bass_kernel_spmd

    a = {k: np.asarray(v) for k, v in inputs.items()}

    def columns(w, widths, blocks):
        k, m = w.shape
        u = w.reshape(k // P, P, m // widths, widths).transpose(2, 1, 0, 3)
        return u.reshape(m // widths, P, blocks, -1).transpose(0, 2, 1, 3)

    def gate_up(w):
        w = w[0].reshape(D, 2, 2, HALF)
        out = np.stack([np.concatenate([columns(w[:, n, f], 2 * P, 2) for n in range(2)], 1) for f in range(2)])
        return out

    def down(w):
        w = w[0].reshape(2, HALF, D)
        return np.stack([columns(w[f], 2 * P, 4).reshape(4, 8, P, -1) for f in range(2)])

    w_in = a["w_in"][0]
    q0, k0, v0, g0, s0 = 0, RH * DK, 2 * RH * DK, 2 * RH * DK + RH * DV, 2 * RH * DK + 2 * RH * DV
    l0 = s0 + 3 * RW
    gr0 = l0 + 128 + 160
    gw0 = gr0 + D
    mix = []
    for h in range(RH):
        steps = [columns(w_in[:, s0 + n * RW + h * 2 * P:s0 + n * RW + (h + 1) * 2 * P], 2 * P, 2)[0] for n in range(3)]
        for c0 in (q0, k0):
            w = w_in[:, c0 + h * DK:c0 + (h + 1) * DK]
            steps.append(columns(np.concatenate([w[:, 0::2], w[:, 1::2]], 1), 2 * P, 2)[0])
        for c0 in (v0, g0):
            w = w_in[:, c0 + h * DV:c0 + (h + 1) * DV]
            steps.append(columns(w[:, 0:2 * P], 2 * P, 2)[0])
            if c0 == v0:
                steps.append(columns(w[:, 2 * P:], 2 * P, 2)[0])
            else:
                steps += [columns(w[:, 2 * P:3 * P], P, 1)[0], columns(w[:, 3 * P:], P, 1)[0]]
        mix.append(np.concatenate(steps, 0))
    w_lora = columns(w_in[:, l0:l0 + 2 * P], 2 * P, 2)[0]
    w_lora2 = np.zeros((1, P, BLK), np.float32)
    w_lora2[0, :, :KT * GATE1] = columns(w_in[:, l0 + 2 * P:gr0], GATE1, 1)[0, 0]
    w_lora = np.concatenate([w_lora, w_lora2], 0)[None]
    w_ro = np.concatenate([columns(w_in[:, gr0:gw0], 2 * P, 2), columns(a["w_ret_o"][0], 2 * P, 2)], 1)
    w_wo = np.zeros((PAIRS, 4, P, BLK), np.float32)
    w_wo[:, 0:2] = columns(w_in[:, gw0:], 2 * P, 2)
    w_wo[:, 2:4, :, :BLK // 2] = columns(a["w_rwkv_o"][0], 2 * P, 2)

    def tiles(v):
        return np.moveaxis(v.reshape(*v.shape[:-1], -1, P), (-1, -2), (0, 1))

    x = np.concatenate([a["x_prompt"].reshape(SEQ, D), a["x_sample"].reshape(NS, D)], 0)
    pp = np.zeros((PAIRS, P, PP), np.float32)
    pp[:, 0:64, 0:P] = a["rwkv_w_up"][0].reshape(64, PAIRS, P).transpose(1, 0, 2)
    pp[:, 64:P, 0:P] = a["rwkv_a_up"][0].reshape(64, PAIRS, P).transpose(1, 0, 2)
    gup = a["rwkv_g_up"][0].reshape(160, PAIRS, P).transpose(1, 0, 2)
    pp[:, :, P:2 * P] = gup[:, 0:P]
    pp[:, 0:GATE1, 2 * P:3 * P] = gup[:, P:]
    shift = a["state_shift"][0]
    pp[:, :, C_SHIFT:C_SHIFT + 3 * SB] = shift[:, :3 * RW].reshape(SB, 3, PAIRS, P).transpose(2, 3, 1, 0).reshape(PAIRS, P, 3 * SB)
    mu = a["rwkv_mu"][0]
    pp[:, :, C_MU:C_MU + 3] = mu[:3 * RW].reshape(3, PAIRS, P).transpose(1, 2, 0)
    for c, name in ((C_W0, "rwkv_w0"), (C_A0, "rwkv_a0"), (C_KK, "rwkv_k_k"), (C_KA, "rwkv_k_a"), (C_RK, "rwkv_r_k"),
                    (C_LNW, "rwkv_ln_w"), (C_LNB, "rwkv_ln_b")):
        pp[:, :, c] = a[name][0].reshape(PAIRS, P)
    lpk = np.zeros((P, 3 * SB + 3), np.float32)
    for k in range(3):
        c = 3 * RW + k * P
        n = min(P, mu.size - c)
        lpk[:n, k * SB:(k + 1) * SB] = shift[:, c:c + n].T
        lpk[:n, 3 * SB + k] = mu[c:c + n]
    gains = np.stack([tiles(a[n].reshape(-1)) for n in ("norm_ffn1", "norm_mix", "norm_ffn2", "norm_final")], 1)
    s_ret = a["state_ret"][0].reshape(SB, RH, P, 2, DV).transpose(1, 0, 2, 3, 4)
    s_rw = a["state_rwkv"][0].reshape(SB, PAIRS, 2, N, N).transpose(1, 2, 4, 0, 3).reshape(PAIRS, P, SB, N)
    arrays = dict(
        x=tiles(x), gu1=gate_up(a["ffn1_w_gu"]), gu2=gate_up(a["ffn2_w_gu"]), down1=down(a["ffn1_w_down"]),
        down2=down(a["ffn2_w_down"]), w_lora=w_lora, w_mix=np.stack(mix), w_ro=w_ro, w_wo=w_wo,
        w_out=columns(a["w_out"][0], 2 * P, 2).reshape(4, 4, P, BLK), gains=gains, pp=pp, lpk=lpk, s_ret=s_ret, s0=s_rw,
        **consts())
    outs = dict(y=(P, KT, T), ret_p=(RH, 2, P, DV), ret_s=(RH, SB, P, 2, DV), rwkv_p=(PAIRS, P, N),
                rwkv_s=(PAIRS, P, SB, N), last_lora=(P, 3, 1 + SB), last=(RH, P, 6, 1 + SB))
    nc = bacc.Bacc("TRN2", target_bir_lowering=False, num_devices=1)
    d, arrs = {}, {}
    for name, v in arrays.items():
        v = np.ascontiguousarray(v)
        arrs[f"in_{name}"] = v
        d[name] = nc.dram_tensor(f"in_{name}", v.shape, F32, kind="ExternalInput").ap()
    for name, shape in outs.items():
        d[name] = nc.dram_tensor(f"out_{name}", shape, F32, kind="ExternalOutput").ap()
    d["spill"] = nc.dram_tensor("spill", (P, KT, T), F32).ap()
    build(nc, d)
    r = run_bass_kernel_spmd(nc, [arrs], core_ids=[0]).results[0]
    o = {name: r[f"out_{name}"] for name in outs}
    y = o["y"].transpose(2, 1, 0).reshape(T, D)
    ret_p = o["ret_p"].transpose(0, 2, 1, 3).reshape(1, 1, RH, DK, DV)
    ret_s = o["ret_s"].reshape(RH, SB, DK, DV).transpose(1, 0, 2, 3)[None]
    rw_p = o["rwkv_p"].reshape(2 * PAIRS, N, N).transpose(0, 2, 1)[None, None]
    rw_s = o["rwkv_s"].reshape(PAIRS, 2, N, SB, N).transpose(3, 0, 1, 4, 2).reshape(1, SB, 2 * PAIRS, N, N)
    main = o["last"].reshape(RH, P, 3, 2, 1 + SB).transpose(4, 2, 0, 3, 1).reshape(1 + SB, 3 * RW)
    low = o["last_lora"].transpose(2, 1, 0).reshape(1 + SB, 3 * P)[:, :288]
    z = np.concatenate([main, low], 1)
    c = np.ascontiguousarray
    return (c(y[:SEQ].reshape(1, SEQ, D)), c(y[SEQ:].reshape(SB, ST, D)), c(ret_p), c(rw_p), c(z[None, 0:1]),
            c(ret_s), c(rw_s), c(z[None, 1:]))
```

```python
from contextlib import ExitStack

import numpy as np

import concourse.bass as bass
from concourse import mybir

F32, F32R = mybir.dt.float32, mybir.dt.float32r
ALU, ACT = mybir.AluOpType, mybir.ActivationFunctionType

P = 128
D = 2048
KT = D // P
FF = 5632
HALF = FF // 2
HT = HALF // P
SEQ, SB, ST = 256, 8, 4
NS = SB * ST
T = SEQ + NS
RH, DK, DV = 4, 256, 512
VT = DV // P
RW = 1024
PAIRS = RW // P
N = 64
CH = 64
BLK = 2048
EPS = 1e-6
GN_EPS = 64e-5
KAPPA = float(np.exp(np.float32(-0.5)))
GATE1 = 160 - P
PP = 3 * P + 3 * SB + 11
C_SHIFT = 3 * P
C_MU = C_SHIFT + 3 * SB
C_W0, C_A0, C_KK, C_KA, C_RK, C_LNW, C_LNB, C_OKA = (C_MU + 3 + n for n in range(8))
RC = 384 + NS + SB * NS + 4
C_QD = 384 + NS
C_KD = C_QD + SB * NS
LEVELS = (2, 4, 8, 16, 32)
SLOTS = 4
LOADS, MIX_LOADS = 4, 8
MIX_BLOCKS, MIX_PAIRS = 18, 10
GATE_PAIRS = 2 * D // (2 * P)
GATE_BLOCKS = 2 * GATE_PAIRS

RET_PE = ("v_turned", "k_turned", "scores", "kv0", "kv1", "o_prompt") + tuple(
    f"kv_s{b}{e}" for b in range(SB) for e in "eo") + ("o_sample_turned", "norm")
RET_ACT = ("v_out", "k_out", "state0", "state1", "o_prompt_out", "o_sample_out", "squared", "root")
RET_DVE = ("v_parts", "q_owned", "masked", "k_parts", "k_owned", "o_sample_back", "done")
RW_PE = ("lora", "kk_sum", "bonus", "turned", "prod_b", "prod_k", "prod_s", "x1") + tuple(
    f"{w}{s}" for s in LEVELS for w in ("y", "d")) + ("nv", "gh") + (
    "upd0", "u1", "upd1", "u2", "upd2", "u3", "upd3", "u_s", "u_s_turned", "upd_s", "out", "mean", "var")
RW_ACT = ("gates", "square", "exps", "root", "turned_out", "eye") + tuple(f"y_out{s}" for s in LEVELS) + (
    "nv_out", "h_out", "us_out", "y_prompt_out", "y_square", "y_root")
RW_DVE = ("summed", "kk_max", "rk", "abk", "bonus", "masked_b", "masked_k", "masked_s", "x1") + tuple(
    f"x{s}" for s in LEVELS) + (
    "g_out", "s1", "u1", "s2", "u2", "s3", "u3", "s4", "u_s", "s_s", "y", "centred", "done")
RW_POOL = ("lm1", "lm_s1", "lm2", "lm_s2") + tuple(f"lm{s}" for s in LEVELS[1:]) + ("k_own", "b_own")

RET_GAPS = (("v_turned", 2), ("k_turned", 1.5), ("scores", 2), ("kv1", 1.5), ("o_prompt", 1.5), ("kv_s3", 4), ("kv_s5", 2),
            ("o_sample", 1.5), ("o_sample_turned", 2), ("norm", 3))
RW_GAPS = (("lora", 3), ("kk_sum", 3), ("kk_root", 3), ("kk_exps", 3), ("turned", 2), ("prod_k", 2), ("prod_s", 3.5),
           ("x1", 2)) + tuple(
    (f"{w}{s}", 1.5) for s in LEVELS for w in ("y", "d")) + (
    ("nv", 1.5), ("gh", 1.5), ("upd0", 1.5), ("u1", 1), ("upd1", 1.5), ("u2", 1), ("upd2", 1.5), ("u3", 1),
    ("upd3", 1.5), ("u_s", 1), ("u_s_turned", 2.5), ("out", 1.5), ("mean", 2.5), ("var", 2))
GAPS = tuple(("ret_" + n, w) for n, w in RET_GAPS) + tuple((f"rw{q}_" + n, w) for q in range(2) for n, w in RW_GAPS)


def quarters(blocks):
    total, seen, out = sum(w for _, w in GAPS), 0, {}
    for name, w in GAPS:
        first = round(4 * blocks * seen / total)
        seen += w
        out[name] = range(first, round(4 * blocks * seen / total))
    return out


def last_block(j):
    return 2 * j + 1 if j < 8 else 8 + j


def build(nc, d):
    with ExitStack() as ctx:
        place = [-(-nc.sbuf_base // 32) * 32]

        def sb(name, shape, dt=F32, at=None):
            size = int(np.prod(shape[1:])) * 4
            offset = place[0] if at is None else at
            if at is None:
                place[0] += -(-size // 32) * 32
            return nc.alloc_sbuf_tensor_at("sb_" + name, list(shape), dt, offset=offset)

        def sem(name):
            return ctx.enter_context(nc.semaphore(name))

        psum = ctx.enter_context(nc.psum_tensor("psum", [P, 8, 512], F32))

        raw = sb("raw", [P, 2, BLK])
        w_hi = sb("w_hi", [P, 2, BLK], F32R)
        w_lo = sb("w_lo", [P, 2, BLK], F32R)
        h_hi = sb("h_hi", [P, KT, T], F32R)
        h_lo = sb("h_lo", [P, KT, T], F32R)
        mean_w = sb("mean_w", [P, P])
        head_w = sb("head_w", [P, P])
        ident = sb("ident", [P, P])
        gains = sb("gains", [P, 4, KT])
        eps_c = sb("eps_c", [P, 2])
        first_root = sb("first_root", [P, 1])
        arena = place[0]

        x = sb("x", [P, KT, T])
        g_hi = sb("g_hi", [P, HT, T], F32R)
        g_lo = sb("g_lo", [P, HT, T], F32R)
        gate = sb("gate", [P, 2, T])
        prod = sb("prod", [P, 2, T])
        sq = sb("sq", [P, 2, T])
        sum_sq = sb("sum_sq", [P, 2, T])
        scale = sb("scale", [P, T])
        ffn_end = place[0]

        place[0] = arena
        o_ret = sb("o_ret", [P, RH * VT, T])
        o_rw = sb("o_rw", [P, PAIRS, T])
        mix = place[0]
        zs_at = place[0]
        zs = sb("zs", [P, 3, 2, 1 + SEQ + SB * (ST + 1)])
        qk = sb("qk", [P, 4, T])
        vg = sb("vg", [P, 2, VT, T])
        lora = sb("lora", [P, 3, T])
        trig = sb("trig", [P, 2, T])
        levels_m = sb("levels_m", [P, 1 + len(LEVELS), P])
        tri = sb("tri", [P, 2, P])
        tri_s = sb("tri_s", [NS, 2, NS])
        own = sb("own", [3 * NS, SB])
        blocks_m = sb("blocks_m", [P, P])
        run_m = sb("run_m", [P, T])
        lpk = sb("lpk", [P, 3 * SB + 3])
        last = sb("last", [P, 6, 1 + SB])
        rot = sb("rot", [P, 2, T])
        units = place[0]
        rc = sb("rc", [P, RC])
        v_tok_at = place[0]
        v_tok = sb("v_tok", [P, 2, DV])
        o_s = sb("o_s", [NS, DV], at=v_tok_at)
        r_scale = sb("r_scale", [P, T], at=v_tok_at + 4 * DV)
        v_tok_s = sb("v_tok_s", [NS, DV])
        v_3 = sb("v_3", [3 * NS, DV], F32R)
        k_tok = sb("k_tok", [P, 2, DK])
        k_s = sb("k_s", [3 * NS, DK])
        k_3 = sb("k_3", [3 * NS, DK], F32R)
        k_own = sb("k_own", [3 * NS, SB, DK], F32R)
        scores = sb("scores", [P, 384 + NS])
        q_own = sb("q_own", [P, 2, SB, NS])
        s_ret = sb("s_ret", [P, SLOTS, 2, DV])
        s_out = sb("s_out", [P, 2, DV])
        ret_end = place[0]
        o_T = vg[:, 0]
        o_sq = qk
        pp2 = sb("pp", [P, 2, PP])
        s0_2 = sb("s0", [P, 2, SB, N])
        rkv2 = sb("rkv", [P, 2, 3, T])
        rkv = rkv2[:, 0]
        top = place[0]
        place[0] = units
        wag = sb("wag", [P, 3, T])
        decays = sb("decays", [P, 3, T])
        csum = sb("csum", [P, 2, T])
        kn = wag[:, 0]
        kk = sb("kk", [P, T])
        ar = sb("ar", [P, 2, T])
        bc = sb("bc", [P, T])
        kc = sb("kc", [P, T])
        ksq = kc
        k2 = sb("k2", [P, T])
        rk = k2
        y_rms = kk
        bonus, ysb, yc = csum[:, 0], decays[:, 1], decays[:, 2]
        tok = sb("tok", [P, 2, 4, P])
        tok_s = sb("tok_s", [NS, 4, P])
        own_at = place[0]
        mt = sb("mt", [P, 4, P])
        nt = sb("nt", [P, 4, P])
        lm = sb("lm", [P, 4, P])
        xm = sb("xm", [P, 4, P])
        b_own = sb("b_own", [NS, SB, P], at=own_at)
        k_own_s = sb("k_own_s", [NS, SB, P], at=own_at + 4 * SB * P)
        pt = sb("pt", [P, 4, P])
        qt = sb("qt", [P, 4, P])
        xt = sb("xt", [P, 4, P])
        ym_at = place[0]
        ym = sb("ym", [P, 4, P])
        nv = sb("nv", [P, 3, P], at=ym_at)
        stt = sb("stt", [P, P], at=ym_at + 12 * P)
        ms = sb("ms", [NS, 4, 2, NS])
        lm_s = sb("lm_s", [NS, 2, NS])
        xm_s = sb("xm_s", [NS, 2, NS])
        xt_s = sb("xt_s", [NS, 2, NS])
        ym_s = sb("ym_s", [NS, 2, NS])
        gm = sb("gm", [P, 3, P])
        hT = sb("hT", [P, 2, P])
        hr = sb("hr", [P, 2, NS])
        um = sb("um", [P, 2, P])
        um_s = sb("um_s", [NS, P])
        st = sb("st", [P, 4, P])
        us = sb("us", [P, 2, NS])
        assert place[0] <= ret_end
        rw_end = top
        gate_z = sb("gate_z", [P, 2, 2, T], at=zs_at)
        place[0] = mix
        or_hi = sb("or_hi", [P, RH * VT, T], F32R)
        or_lo = sb("or_lo", [P, RH * VT, T], F32R)
        part = sb("part", [P, KT, T])
        place[0] = arena
        ow_at = mix + 12 * KT * T + 24 * T
        ow_hi = sb("ow_hi", [P, PAIRS, T], F32R, at=ow_at)
        ow_lo = sb("ow_lo", [P, PAIRS, T], F32R, at=ow_at + 4 * PAIRS * T)
        mg_at = mix
        m_hi = sb("m_hi", [P, KT, T], F32R, at=mg_at)
        m_lo = sb("m_lo", [P, KT, T], F32R, at=mg_at + 4 * KT * T)
        gate_m = sb("gate_m", [P, 2, 2, T], at=mix + 12 * KT * T)
        prod_m = sb("prod_m", [P, 2, T], at=mix + 12 * KT * T + 16 * T)
        assert max(ffn_end, ret_end, rw_end, ow_at + 8 * PAIRS * T) <= nc.sbuf_usable_end

        raw_landed = [sem("raw_landed0"), sem("raw_landed1")]
        hi_made, lo_made = sem("hi_made"), sem("lo_made")
        used = sem("used")
        psum_free = [sem("psum_free0"), sem("psum_free1")]
        loaded, mix_loaded = sem("loaded"), sem("mix_loaded")
        spilled, x_back = sem("spilled"), sem("x_back")
        eps_made = sem("eps_made")
        x_landed = [sem(f"x_landed{n}") for n in range(4)]
        act_chain, dve_chain = sem("act_chain"), sem("dve_chain")
        squares, mean_made, root_made = sem("squares"), sem("mean_made"), sem("root_made")
        normed, normed_hi, normed_lo = sem("normed"), sem("normed_hi"), sem("normed_lo")
        gate_made, gate_used = sem("gate_made"), sem("gate_used")
        hidden, hidden_hi, hidden_lo = sem("hidden"), sem("hidden_hi"), sem("hidden_lo")
        merged, merged_hi, merged_lo = sem("merged"), sem("merged_hi"), sem("merged_lo")
        o_hi, o_lo = sem("o_hi"), sem("o_lo")
        lora_shifted, lora_made = sem("lora_shifted"), sem("lora_made")
        last_made, last_sent = sem("last_made"), sem("last_sent")
        ret_pe, ret_act, ret_dve = sem("ret_pe"), sem("ret_act"), sem("ret_dve")
        rw_pe, rw_act, rw_dve, rw_pool = sem("rw_pe"), sem("rw_act"), sem("rw_dve"), sem("rw_pool")
        rc_landed = sem("rc_landed")
        pp_landed = [sem("pp_landed0"), sem("pp_landed1")]
        zs_used = sem("zs_used")
        gate_z_made = sem("gate_z_made")
        gate_z_sent = [sem("gate_z_sent0"), sem("gate_z_sent1")]
        gate_back = [sem("gate_back0"), sem("gate_back1")]
        s_landed = [sem(f"s_landed{i}") for i in range(SLOTS)]
        s_sent = [sem(f"s_sent{i}") for i in range(SLOTS)]
        s_new = sem("s_new")
        rp_sent = sem("rp_sent")
        wp_sent = [sem("wp_sent0"), sem("wp_sent1")]
        ws_sent = [sem("ws_sent0"), sem("ws_sent1")]
        stored = sem("stored")
        parted = sem("parted")

        def at(steps, name, unit):
            return unit * len(steps) + (steps.index(name) + 1)

        def is_first(i):
            return isinstance(i, int) and i == 0

        def wait(eng, s, value):
            if not (isinstance(value, int) and value <= 0):
                eng.wait_ge(s, value)

        def loop(eng, count, body):
            body(0)
            if count > 1:
                with eng.Fori(1, count) as i:
                    body(i)

        class Chain:

            def __init__(self, eng, s):
                self.eng, self.s, self.n, self.base = eng, s, 0, 0

            def do(self, ins, wait=True):
                ins.then_inc(self.s, 1)
                self.n += 1
                if wait:
                    self.eng.wait_ge(self.s, self.base + self.n)

            def loop(self, count, body, per=None):
                before = self.n
                body(0)
                per, start = self.n - before if per is None else per, self.n
                if count > 1:
                    with self.eng.Fori(1, count) as i:
                        self.base = (i - 1) * per
                        body(i)
                        assert self.n - start == per, (self.n - start, per)
                    self.base, self.n = 0, start + per * (count - 1)

        taken = [0, 0]

        def phase(nb, npairs, times):
            b, g = taken
            taken[0] += nb * times
            taken[1] += npairs * times
            return b, g

        ffn = []
        for n in range(2):
            if n:
                lora_ph = phase(3, 2, 1)
                mix_ph = phase(MIX_BLOCKS, MIX_PAIRS, RH)
                gates_ph = phase(GATE_BLOCKS, GATE_PAIRS, 1)
                ret_o_ph = phase(4, 2, PAIRS // 2)
                rw_o_ph = phase(2, 2, PAIRS // 2)
                w_out_ph = phase(4, 2, 4)
            ffn.append([(phase(4, 2, HT // 2), phase(8, 2, 4)) for _ in range(2)])
        next_ph = (mix_ph[0] + MIX_BLOCKS, mix_ph[1] + MIX_PAIRS)
        DOWN = HT * P // 2
        LORA2 = KT * GATE1

        def units_free_of_retention(eng, i):
            eng.wait_ge(rp_sent, i * 32 + 32)
            for s in s_sent:
                eng.wait_ge(s, i * (16 * SB // SLOTS) + 16 * SB // SLOTS)

        def units_free_of_rwkv(eng, i):
            eng.wait_ge(rw_dve, i * (2 * len(RW_DVE)) + 2 * len(RW_DVE))
            for s in wp_sent:
                eng.wait_ge(s, i * 32 + 32)

        def mixing_over(eng):
            units_free_of_rwkv(eng, RH - 1)
            for s in ws_sent:
                eng.wait_ge(s, RH * 16)
            for s in gate_z_sent:
                eng.wait_ge(s, 8 * GATE_PAIRS)
            eng.wait_ge(last_sent, 16 * (RH + 1))

        class Weave:

            def __init__(self, blocks, quarter):
                self.share, self.quarter, self.left = quarters(blocks), quarter, [n for n, _ in GAPS]

            def __call__(self, gap):
                assert self.left.pop(0) == gap, gap
                for n in self.share[gap]:
                    self.quarter(*divmod(n, 4))

        def mixed_in(eng, i):
            for s in range(2):
                eng.wait_ge(psum_free[s], i * 5 + (mix_ph[1] // 2 + 5))

        block = ctx.enter_context(nc.Block())

        @block.sync
        def _(sp):
            def load(n, first, src, cols=BLK):
                wait(sp, lo_made, n + (first - 1))
                sp.dma_start(raw[:, first % 2, 0:cols], src).then_inc(raw_landed[first % 2], 16)

            def run(ph, times, src, widths):
                def body(i):
                    for j, cols in enumerate(widths):
                        load(i * len(widths), ph[0] + j, src[i, j, :, 0:cols], cols)
                loop(sp, times, body)

            def feed(n, gu, down):
                for f in range(2):
                    run(ffn[n][f][0], HT // 2, gu[f], [BLK] * 4)
                    run(ffn[n][f][1], 4, down[f], [DOWN] * 8)

            feed(0, d["gu1"], d["down1"])
            run(lora_ph, 1, d["w_lora"], [BLK, BLK, LORA2])
            run(mix_ph, RH, d["w_mix"], [BLK] * MIX_BLOCKS)

            def store_gate(j):
                sp.wait_ge(gate_z_made, j + 1)
                sp.dma_start(d["gates"][j // PAIRS, j % PAIRS // 2, j % 2], gate_z[:, j % 2, :, :]).then_inc(gate_z_sent[j % 2], 16)

            for n in range(GATE_BLOCKS):
                load(0, gates_ph[0] + n, d["w_gates"][n])
                if n >= 5 and n % 2:
                    store_gate((n - 5) // 2)
            for j in range(2):
                load(0, ret_o_ph[0] + j, d["w_ro"][0, j])
                store_gate(GATE_PAIRS - 2 + j)
            mixing_over(sp)

            def load_gate(i, j, n):
                wait(sp, gate_used, i * 2 + (n * PAIRS + j - 1))
                sp.dma_start(gate_m[:, j, :, :], d["gates"][n, i, j]).then_inc(gate_back[j], 16)

            def ret_o(i):
                for j in range(4):
                    if j >= 2 or not is_first(i):
                        load(i * 4, ret_o_ph[0] + j, d["w_ro"][i, j])
                    if j % 2 == 0:
                        load_gate(i, j // 2, 0)
            loop(sp, PAIRS // 2, ret_o)

            def rw_o(i):
                for j in range(2):
                    load(i * 2, rw_o_ph[0] + j, d["w_wo"][i, j])
                    load_gate(i, j, 1)
            loop(sp, PAIRS // 2, rw_o)
            run(w_out_ph, 4, d["w_out"], [BLK] * 4)
            feed(1, d["gu2"], d["down2"])
            for k in range(0, KT, 4):
                sp.wait_ge(normed, 3 * KT + k + 4)
                sp.dma_start(d["y"][:, k:k + 4, :], x[:, k:k + 4, :]).then_inc(stored, 16)
            sp.wait_ge(stored, 16 * (KT // 4))

        @block.tensor
        def _(pe):
            def products(out, wh, wl, xh, xl, start, stop):
                pe.matmul(out, wh, xh, start=start, stop=False)
                pe.matmul(out, wh, xl, start=False, stop=False)
                return pe.matmul(out, wl, xh, start=False, stop=stop)

            def pair(i, ph, j, g, nblk, nk, hi, lo, widths=(P, P), ready=None):
                b0, g0, bs, gs = ph
                pe.wait_ge(psum_free[(g0 + g) % 2], i * (gs // 2) + (g0 + g) // 2)
                per = nk * len(widths) // nblk
                u = 0
                for jj in range(j, j + nblk):
                    pe.wait_ge(lo_made, i * bs + (b0 + jj + 1))
                    slot = (b0 + jj) % 2
                    col = 0
                    for _ in range(per):
                        k, m = divmod(u, len(widths))
                        w = widths[m]
                        if ready is not None and m == 0:
                            pe.wait_ge(*ready(k))
                        mm = products(psum[0:w, 2 * ((g0 + g) % 2) + m, 0:T],
                                      w_hi[:, slot, col:col + w], w_lo[:, slot, col:col + w],
                                      hi[:, k, :], lo[:, k, :], k == 0, k == nk - 1)
                        col += w
                        u += 1
                    mm.then_inc(used, 1)

            def norm(r):
                pe.wait_ge(squares, r + 1)
                for k in range(2):
                    mm = pe.matmul(psum[:, 4, 0:T], mean_w[:, :], sum_sq[:, k, :], start=(k == 0), stop=(k == 1))
                mm.then_inc(mean_made, 1)

            pe.wait_ge(loaded, 16 * LOADS)

            def normed_by(r):
                return lambda k: (normed_lo, r * KT + k + 1)

            def feed(n):
                norm(2 * n)
                for f in range(2):
                    up_ph, down_ph = (*ffn[n][f][0], 4, 2), (*ffn[n][f][1], 8, 2)

                    def up(i):
                        pair(i, up_ph, 0, 0, 2, KT, h_hi, h_lo, ready=normed_by(2 * n) if is_first(i) and f == 0 else None)
                        pair(i, up_ph, 2, 1, 2, KT, h_hi, h_lo)
                    loop(pe, HT // 2, up)
                    done = (2 * n + f) * (HT // 2)

                    def down(i):
                        pair(i, down_ph, 0, 0, 4, HT, g_hi, g_lo,
                             ready=(lambda k: (hidden_lo, done + k // 2 + 1)) if is_first(i) else None)
                        pair(i, down_ph, 4, 1, 4, HT, g_hi, g_lo)
                    loop(pe, 4, down)

            feed(0)
            norm(1)
            pair(0, (*lora_ph, 3, 2), 0, 0, 2, KT, h_hi, h_lo, ready=normed_by(1))
            pair(0, (*lora_ph, 3, 2), 2, 1, 1, KT, h_hi, h_lo, widths=(GATE1,))

            def projections(i):
                for n in range(MIX_BLOCKS):
                    for q in range(4):
                        quarter(i, (*mix_ph, MIX_BLOCKS, MIX_PAIRS), n, q)

            def quarter(i, ph, n, q):
                b0, g0, bs, gs = ph
                single = bs == MIX_BLOCKS and n >= 16
                g = g0 + (n - 8 if single else n // 2)
                if q == 0:
                    if single or n % 2 == 0:
                        pe.wait_ge(psum_free[g % 2], i * (gs // 2) + g // 2)
                    pe.wait_ge(lo_made, i * bs + (b0 + n + 1))
                slot = (b0 + n) % 2
                for u in range(4 * q, 4 * q + 4):
                    k, m = (u, 0) if single else divmod(16 * (n % 2) + u, 2)
                    mm = products(psum[:, 2 * (g % 2) + m, 0:T], w_hi[:, slot, u * P:(u + 1) * P],
                                  w_lo[:, slot, u * P:(u + 1) * P], h_hi[:, k, :], h_lo[:, k, :], k == 0, k == KT - 1)
                if q == 3:
                    mm.then_inc(used, 1)

            def transpose(out, in_, n=P):
                return pe.transpose(out, in_, ident[0:n, 0:n])

            def retention(h, weave):
                def step(mm):
                    mm.then_inc(ret_pe, 1)

                def after(s, steps, name):
                    pe.wait_ge(s, at(steps, name, h))
                mixed_in(pe, h)
                wait(pe, rw_act, h * (2 * len(RW_ACT)))
                for tt in range(2):
                    for m in range(VT):
                        mm = transpose(psum[:, 4 + tt, m * P:(m + 1) * P], vg[:, 0, m, tt * P:(tt + 1) * P])
                for m in range(VT):
                    for n in range(3):
                        mm = pe.matmul(psum[n * NS:(n + 1) * NS, 6, m * P:(m + 1) * P], vg[:, 0, m, SEQ:T], ident[:, :],
                                       start=True, stop=True)
                step(mm)
                weave("ret_v_turned")
                for tt in range(2):
                    for e in range(2):
                        mm = transpose(psum[:, 7, (2 * tt + e) * P:(2 * tt + e + 1) * P], qk[:, 2 + e, tt * P:(tt + 1) * P])
                after(ret_act, RET_ACT, "v_out")
                after(ret_dve, RET_DVE, "v_parts")
                for e in range(2):
                    for n in range(3):
                        mm = pe.matmul(psum[n * NS:(n + 1) * NS, 6, e * P:(e + 1) * P], qk[:, 2 + e, SEQ:T], ident[:, :],
                                       start=True, stop=True)
                step(mm)
                weave("ret_k_turned")
                for e in range(2):
                    pe.matmul(psum[:, 4, 0:SEQ], qk[:, 2 + e, 0:P], qk[:, e, 0:SEQ], start=(e == 0), stop=(e == 1))
                for e in range(2):
                    pe.matmul(psum[:, 5, 0:P], qk[:, 2 + e, P:SEQ], qk[:, e, P:SEQ], start=(e == 0), stop=(e == 1))
                for e in range(2):
                    mm = pe.matmul(psum[0:NS, 5, P:P + NS], qk[:, 2 + e, SEQ:T], qk[:, e, SEQ:T], start=(e == 0),
                                   stop=(e == 1), skip_group_check=True)
                step(mm)
                weave("ret_scores")
                after(ret_act, RET_ACT, "k_out")
                for e in range(2):
                    for tt in range(2):
                        mm = pe.matmul(psum[:, 6 + e, :], k_tok[:, tt, e * P:(e + 1) * P], v_tok[:, tt, :],
                                       start=(tt == 0), stop=(tt == 1))
                    step(mm)
                weave("ret_kv1")
                after(ret_dve, RET_DVE, "masked")
                for m in range(VT):
                    out = psum[:, 4 + m // 2, (m % 2) * SEQ:(m % 2 + 1) * SEQ]
                    pe.matmul(out, v_tok[:, 0, m * P:(m + 1) * P], scores[:, 0:SEQ], start=(m % 2 == 0), stop=False,
                              skip_group_check=True)
                    mm = pe.matmul(out[:, P:SEQ], v_tok[:, 1, m * P:(m + 1) * P], scores[:, SEQ:384], start=False,
                                   stop=True, skip_group_check=True)
                step(mm)
                weave("ret_o_prompt")
                after(ret_dve, RET_DVE, "q_owned")
                after(ret_act, RET_ACT, "state0")
                pe.sem_inc(parted, 1)
                pe.matmul(psum[0:NS, 6, :], scores[0:NS, 384:384 + NS], v_tok_s[:, :], start=True, stop=False)
                after(ret_act, RET_ACT, "state1")
                after(ret_act, RET_ACT, "o_prompt_out")
                after(ret_dve, RET_DVE, "k_owned")
                for bb in range(SB):
                    slot = bb % SLOTS
                    pe.wait_ge(s_landed[slot], h * (16 * SB // SLOTS) + 16 * (bb // SLOTS + 1))
                    for e in range(2):
                        mm = pe.matmul(psum[0:NS, 6, :], q_own[:, e, bb, :], s_ret[:, slot, e, :],
                                       start=False, stop=(bb == SB - 1 and e == 1))
                    for e in range(2):
                        u = 2 * bb + e
                        if u >= 3:
                            pe.wait_ge(s_new, h * (2 * SB) + (u - 2))
                        step(pe.matmul(psum[:, (7, 4, 5)[u % 3], :], k_own[:, bb, e * P:(e + 1) * P], v_3[:, :],
                                       start=True, stop=True))
                    if bb in (3, 5):
                        weave(f"ret_kv_s{bb}")
                weave("ret_o_sample")
                after(ret_act, RET_ACT, "o_sample_out")
                pe.sem_inc(parted, 1)
                for m in range(VT):
                    mm = transpose(psum[:, 6, m * NS:(m + 1) * NS], o_s[:, m * P:(m + 1) * P], NS)
                step(mm)
                weave("ret_o_sample_turned")
                after(ret_act, RET_ACT, "squared")
                for m in range(VT):
                    mm = pe.matmul(psum[:, 7, 0:T], mean_w[:, :], o_sq[:, m, :], start=(m == 0), stop=(m == VT - 1))
                step(mm)
                weave("ret_norm")

            def rwkv(p, q, weave):
                pp, rkv, s0 = pp2[:, q], rkv2[:, q], s0_2[:, q]
                gap = f"rw{q}_"

                def step(mm):
                    mm.then_inc(rw_pe, 1)

                def after(s, steps, name):
                    pe.wait_ge(s, at(steps, name, p))
                wait(pe, rw_act, p * len(RW_ACT))
                pe.wait_ge(pp_landed[q], (p - q) * 16 + 32)
                pe.matmul(psum[:, 4, 0:T], pp[0:64, 0:P], lora[0:64, 0, :], start=True, stop=True)
                pe.matmul(psum[:, 5, 0:T], pp[64:P, 0:P], lora[64:P, 0, :], start=True, stop=True)
                pe.matmul(psum[:, 6, 0:T], pp[:, P:2 * P], lora[:, 1, :], start=True, stop=False)
                step(pe.matmul(psum[:, 6, 0:T], pp[0:GATE1, 2 * P:3 * P], lora[0:GATE1, 2, :], start=False, stop=True))
                weave(gap + "lora")
                after(rw_act, RW_ACT, "square")
                step(pe.matmul(psum[:, 7, 0:T], head_w[:, :], ksq[:, :], start=True, stop=True))
                for part in ("kk_sum", "kk_root"):
                    weave(gap + part)
                after(rw_dve, RW_DVE, "rk")
                step(pe.matmul(psum[:, 7, 0:T], head_w[:, :], rk[:, :], start=True, stop=True))
                weave(gap + "kk_exps")
                src = [ar[:, 0], bc[:, :], kc[:, :], rkv[:, 2]]
                for n in (3, 2, 0, 1):
                    if n == 0:
                        after(rw_dve, RW_DVE, "abk")
                    for tt in range(2):
                        transpose(psum[:, 4 + tt, n * P:(n + 1) * P], src[n][:, tt * P:(tt + 1) * P])
                    mm = transpose(psum[0:NS, 6, n * P:(n + 1) * P], src[n][:, SEQ:T])
                step(mm)
                weave(gap + "turned")
                after(rw_act, RW_ACT, "turned_out")
                for n, s in enumerate((bc, kc)):
                    if n:
                        after(rw_dve, RW_DVE, "bonus")
                    for hd in range(2):
                        r = slice(64 * hd, 64 * hd + 64)
                        for tt in range(2):
                            cols = slice(tt * P, (tt + 1) * P)
                            mm = pe.matmul(psum[:, 4 + 2 * n + hd, tt * 256:tt * 256 + 256], s[r, cols], ar[r, :, cols],
                                           start=True, stop=True, skip_group_check=True)
                    step(mm)
                weave(gap + "prod_k")
                after(rw_dve, RW_DVE, "masked_b")
                pe.sem_inc(parted, 1)
                for hd in range(2):
                    r = slice(64 * hd, 64 * hd + 64)
                    for n, s in enumerate((bc, kc)):
                        c = n * 2 * NS
                        mm = pe.matmul(psum[0:NS, 4 + hd, c:c + 2 * NS], s[r, SEQ:T], ar[r, :, SEQ:T],
                                       start=True, stop=True, skip_group_check=True)
                step(mm)
                weave(gap + "prod_s")
                after(rw_dve, RW_DVE, "masked_s")
                after(rw_act, RW_ACT, "eye")
                after(rw_pool, RW_POOL, "lm_s1")
                ev = ident[:, :].rearrange("p (b two) -> p b two", two=2)[:, :, 0]
                for t in range(4):
                    mm = pe.matmul(psum[:, 5, t * 64:(t + 1) * 64], lm[:, t, :], ev, start=True, stop=True)
                for hd in range(2):
                    mm = pe.matmul(psum[0:NS, 5, 256 + hd * 16:272 + hd * 16], lm_s[:, hd, :], ev[0:NS, 0:16],
                                   start=True, stop=True)
                step(mm)
                weave(gap + "x1")
                before = "x1"
                for s in LEVELS:
                    after(rw_pool, RW_POOL, f"lm{s}" if s > 2 else "lm_s2")
                    after(rw_dve, RW_DVE, before)
                    for t in range(4):
                        mm = pe.matmul(psum[:, 5, t * P:(t + 1) * P], lm[:, t, :], xm[:, t, :], start=True, stop=True)
                    if s == 2:
                        for hd in range(2):
                            mm = pe.matmul(psum[0:NS, 4, hd * NS:(hd + 1) * NS], lm_s[:, hd, :], xm_s[:, hd, :],
                                           start=True, stop=True)
                    step(mm)
                    weave(gap + f"y{s}")
                    after(rw_act, RW_ACT, f"y_out{s}")
                    for t in range(4):
                        y1 = ym[:, t, :].rearrange("p (b two s) -> p b two s", two=2, s=s)[:, :, 0, :]
                        x2 = xt[:, t, :].rearrange("p (b two s) -> p b two s", two=2, s=s)[:, :, 1, :]
                        if s < 32:
                            pe.matmul(psum[:, 6, t * 64:(t + 1) * 64], xt[:, t, :], y1, start=True, stop=True)
                        mm = pe.matmul(psum[:, 7, t * 64:(t + 1) * 64], ym[:, t, :], x2, start=True, stop=True)
                    if s == 2:
                        for hd in range(2):
                            x2 = xt_s[:, hd, :].rearrange("p (b two s) -> p b two s", two=2, s=s)[:, :, 1, :]
                            mm = pe.matmul(psum[0:NS, 7, 256 + hd * 16:272 + hd * 16], ym_s[:, hd, :], x2,
                                           start=True, stop=True)
                    step(mm)
                    weave(gap + f"d{s}")
                    before = f"x{s}"
                after(rw_dve, RW_DVE, f"x{LEVELS[-1]}")
                for hd in range(2):
                    v = slice(64 * hd, 64 * hd + 64)
                    for tt in range(2):
                        pe.matmul(psum[:, 4, tt * P + hd * 64:tt * P + hd * 64 + 64], nt[:, 2 * hd + tt, :],
                                  tok[:, tt, 3, v], start=True, stop=True)
                    mm = pe.matmul(psum[0:NS, 4, 256 + hd * 64:320 + hd * 64], ms[:, 2 * hd + 1, 0, :], tok_s[:, 3, v],
                                   start=True, stop=True)
                step(mm)
                weave(gap + "nv")
                after(rw_act, RW_ACT, "nv_out")
                for hd in range(2):
                    v = slice(64 * hd, 64 * hd + 64)
                    for tt in range(2):
                        pe.matmul(psum[:, 5, tt * P + hd * 64:tt * P + hd * 64 + 64], xt[:, 2 * hd + tt, :], nv[:, tt, v],
                                  start=True, stop=True)
                        pe.matmul(psum[v, 6, tt * P:(tt + 1) * P], tok[:, tt, 0, v], xt[:, 2 * hd + tt, :],
                                  start=True, stop=True)
                    pe.matmul(psum[0:NS, 5, 256 + hd * 64:320 + hd * 64], xt_s[:, hd, :], nv[0:NS, 2, v],
                              start=True, stop=True)
                    mm = pe.matmul(psum[v, 6, 256:256 + NS], tok_s[:, 0, v], xt_s[:, hd, :], start=True, stop=True)
                step(mm)
                weave(gap + "gh")
                for c in range(4):
                    tt, off = divmod(c * CH, P)
                    r = slice(off, off + CH)
                    if c == 0:
                        after(rw_dve, RW_DVE, "g_out")
                        after(rw_act, RW_ACT, "h_out")
                    else:
                        after(rw_dve, RW_DVE, f"s{c}")
                        step(pe.matmul(psum[r, 4, 0:P], hT[:, tt, r], st[:, c - 1, :], start=True, stop=True))
                        weave(gap + f"u{c}")
                        after(rw_dve, RW_DVE, f"u{c}")
                    pe.matmul(psum[:, 7, 0:P], tok[r, tt, 1, :], um[r, tt, :], start=True, stop=False)
                    step(pe.matmul(psum[:, 7, 0:P], tok[r, tt, 2, :], tok[r, tt, 3, :], start=False, stop=True))
                    weave(gap + f"upd{c}")
                for bb in range(SB):
                    for hd in range(2):
                        v = slice(64 * hd, 64 * hd + 64)
                        mm = pe.matmul(psum[v, 5, bb * 8:bb * 8 + 8], s0[v, bb, :], hr[v, :, bb * ST:(bb + 1) * ST],
                                       start=True, stop=True, skip_group_check=True)
                step(mm)
                weave(gap + "u_s")
                after(rw_act, RW_ACT, "us_out")
                step(transpose(psum[0:NS, 6, 0:P], us[:, 0, :]))
                weave(gap + "u_s_turned")
                after(rw_pool, RW_POOL, "b_own")
                after(rw_dve, RW_DVE, "u_s")
                for bb in range(SB):
                    out = psum[:, 4 + bb // 4, bb % 4 * P:(bb % 4 + 1) * P]
                    pe.matmul(out, k_own_s[:, bb, :], tok_s[:, 3, :], start=True, stop=False, skip_group_check=True)
                    mm = pe.matmul(out, b_own[:, bb, :], um_s[:, :], start=False, stop=True, skip_group_check=True)
                step(mm)
                after(rw_dve, RW_DVE, "s4")
                for tt in range(2):
                    for hd in range(2):
                        v = slice(64 * hd, 64 * hd + 64)
                        pe.matmul(psum[v, 7, tt * P:(tt + 1) * P], tok[:, tt, 3, v], qt[:, 2 * hd + tt, :],
                                  start=(tt == 0), stop=False, skip_group_check=True)
                        pe.matmul(psum[v, 7, tt * P:(tt + 1) * P], um[:, tt, v], pt[:, 2 * hd + tt, :],
                                  start=False, stop=False, skip_group_check=True)
                for c in range(1, 4):
                    pe.matmul(psum[:, 7, c * CH:(c + 1) * CH], st[:, c - 1, :], ar[:, 1, c * CH:(c + 1) * CH],
                              start=False, stop=True, skip_group_check=True)
                for hd in range(2):
                    v = slice(64 * hd, 64 * hd + 64)
                    pe.matmul(psum[v, 7, SEQ:T], tok_s[:, 3, v], ms[:, 2 * hd + 1, 1, :], start=False, stop=False,
                              skip_group_check=True)
                    mm = pe.matmul(psum[v, 7, SEQ:T], um_s[:, v], ms[:, 2 * hd, 1, :], start=False, stop=True,
                                   skip_group_check=True)
                step(mm)
                weave(gap + "out")
                after(rw_dve, RW_DVE, "y")
                step(pe.matmul(psum[:, 6, 0:T], head_w[:, :], ysb, start=True, stop=True))
                weave(gap + "mean")
                after(rw_act, RW_ACT, "y_square")
                step(pe.matmul(psum[:, 4, 0:T], head_w[:, :], ksq[:, :], start=True, stop=True))
                weave(gap + "var")

            projections(0)
            pe.wait_ge(lora_made, 1)
            pe.wait_ge(mix_loaded, 16 * MIX_LOADS)

            def units_of(i, weave):
                retention(i, weave)
                pe.wait_ge(ret_act, at(RET_ACT, "root", i))
                for q in range(2):
                    rwkv(i * 2 + q, q, weave)

            with pe.Fori(0, RH - 1) as i:
                units_of(i, Weave(MIX_BLOCKS, lambda n, q: quarter(i, (*next_ph, MIX_BLOCKS, MIX_PAIRS), n, q)))
            units_of(RH - 1, Weave(GATE_BLOCKS, lambda n, q: quarter(0, (*gates_ph, GATE_BLOCKS, GATE_PAIRS), n, q)))


            def ret_o(i):
                for j in range(2):
                    pair(i, (*ret_o_ph, 4, 2), 2 * j, j, 2, KT, or_hi, or_lo,
                         ready=(lambda k: (o_lo, k + 1)) if is_first(i) and j == 0 else None)
            loop(pe, PAIRS // 2, ret_o)

            def rw_o(i):
                for j in range(2):
                    pair(i, (*rw_o_ph, 2, 2), j, j, 1, PAIRS, ow_hi, ow_lo,
                         ready=(lambda k: (o_lo, RH * VT + k + 1)) if is_first(i) and j == 0 else None)
            loop(pe, PAIRS // 2, rw_o)

            def out(i):
                for j in range(2):
                    pair(i, (*w_out_ph, 4, 2), 2 * j, j, 2, KT, m_hi, m_lo,
                         ready=(lambda k: (merged_lo, k // 2 + 1)) if is_first(i) and j == 0 else None)
            loop(pe, 4, out)
            feed(1)
            norm(3)

        @block.scalar
        def _(act):
            ch = Chain(act, act_chain)

            def split(n, first, cols=BLK):
                slot = first % 2
                act.wait_ge(raw_landed[slot], n * 8 + 16 * (first // 2 + 1))
                wait(act, used, n + (first - 1))
                act.activation(w_hi[:, slot, 0:cols], raw[:, slot, 0:cols], ACT.Copy).then_inc(hi_made, 1)

            def norm(r, first=None):
                if first is not None:
                    split(0, first)
                    split(0, first + 1)
                act.activation(first_root[:, :], eps_c[:, 0:1], ACT.Sqrt)
                act.wait_ge(mean_made, r + 1)
                act.activation(scale[:, :], psum[:, 4, 0:T], ACT.Sqrt, bias=eps_c[:, 0:1]).then_inc(root_made, 1)
                if r < 3:
                    for k in range(KT):
                        act.wait_ge(normed, r * KT + k + 1)
                        act.activation(h_hi[:, k, :], prod[:, k % 2, :], ACT.Copy).then_inc(normed_hi, 1)

            act.wait_ge(eps_made, 1)

            def feed(n):
                norm(2 * n, ffn[n][0][0][0])
                for f in range(2):
                    (b, g), (bd, _) = ffn[n][f]
                    done = (2 * n + f) * (HT // 2)
                    gates = done

                    def hidden_part(i):
                        act.wait_ge(hidden, i + (done + 1))
                        act.activation(g_hi[:, bass.ds(i * 2, 2), :], prod[:, :, :], ACT.Copy).then_inc(hidden_hi, 1)

                    def up(i):
                        if f or not is_first(i):
                            split(i * 4, b)
                            split(i * 4, b + 1)
                        if not is_first(i):
                            hidden_part(i - 1)
                        split(i * 4, b + 2)
                        split(i * 4, b + 3)
                        act.wait_ge(used, i * 4 + (b + 2))
                        wait(act, hidden, i + done)
                        act.activation(gate[:, :, :], psum[:, 2 * (g % 2):2 * (g % 2) + 2, 0:T],
                                       ACT.Silu).then_inc(gate_made, 1)
                        act.wait_ge(gate_made, i + (gates + 1))
                        act.sem_inc(psum_free[g % 2], 1)
                    loop(act, HT // 2, up)
                    split(0, bd, DOWN)
                    hidden_part(HT // 2 - 1)

                    def down(i):
                        for j in range(8):
                            if j or not is_first(i):
                                split(i * 8, bd + j, DOWN)
                    loop(act, 4, down)

            feed(0)
            b, g = lora_ph
            norm(1, b)
            split(0, b + 2, LORA2)
            split(0, mix_ph[0])
            split(0, mix_ph[0] + 1)

            def z_copy(dst, tiles, g, w=P):
                s = 2 * (g % 2)
                ch.do(act.activation(dst[0:w, 0:tiles, 1:1 + SEQ], psum[0:w, s:s + tiles, 0:SEQ], ACT.Copy), wait=False)
                sample = dst[0:w, 0:tiles, 1 + SEQ:].rearrange("p a (b t) -> p a b t", t=ST + 1)
                for a in range(tiles):
                    ins = act.activation(sample[:, a, :, 1:], psum[0:w, s + a, SEQ:T].rearrange("p (b t) -> p b t", t=ST),
                                         ACT.Copy)
                    if a < tiles - 1:
                        ch.do(ins, wait=False)
                ins.then_inc(psum_free[g % 2], 1)

            act.wait_ge(used, b + 2)
            z_copy(zs[:, 0], 2, g)
            act.wait_ge(used, b + 3)
            z_copy(zs[:, 1], 1, g + 1, GATE1)
            act.wait_ge(lora_shifted, 1)
            ch.do(act.activation(lora[0:64, 0, :], rkv[0:64, 0, :], ACT.Tanh), wait=False)
            ch.do(act.activation(lora[64:P, 0, :], rkv[64:P, 0, :], ACT.Copy), wait=False)
            ch.do(act.activation(lora[:, 1, :], rkv[:, 1, :], ACT.Sigmoid), wait=False)
            act.activation(lora[0:GATE1, 2, :], rkv[0:GATE1, 2, :], ACT.Sigmoid).then_inc(lora_made, 1)
            act.wait_ge(lora_made, 1)

            def read_out(i, ph, j):
                if j in (3, 4):
                    return
                b, g = ph
                act.wait_ge(used, i * MIX_BLOCKS + (b + last_block(j) + 1))
                s = 2 * ((g + j) % 2)
                if j < 3:
                    return z_copy(zs[:, j], 2, g + j)
                elif j < 7:
                    ins = act.activation(vg[:, 0, 2 * (j - 5):2 * (j - 5) + 2, :], psum[:, s:s + 2, 0:T], ACT.Copy)
                elif j == 7:
                    ins = act.activation(vg[:, 1, 0:2, :], psum[:, s:s + 2, 0:T], ACT.Silu)
                else:
                    ins = act.activation(vg[:, 1, j - 6, :], psum[:, s, 0:T], ACT.Silu)
                ins.then_inc(psum_free[(g + j) % 2], 1)

            def quarter(i, ph, n, q):
                if q == 0:
                    split(i * MIX_BLOCKS, ph[0] + n + 1)
                if q == 3:
                    for j in range(MIX_PAIRS):
                        if last_block(j) == n:
                            read_out(i, ph, j)

            def gates_quarter(n, q):
                b, g = gates_ph
                if q == 0:
                    split(0, b + n + 1)
                if q == 3 and n % 2 == 1:
                    j = n // 2
                    if j < 2:
                        act.wait_ge(zs_used, RH)
                    act.wait_ge(used, b + n + 1)
                    wait(act, gate_z_sent[j % 2], 16 * (j // 2))
                    s = 2 * ((g + j) % 2)
                    act.activation(gate_z[:, j % 2, :, :], psum[:, s:s + 2, 0:T], ACT.Sigmoid).then_inc(gate_z_made, 1)
                    act.wait_ge(gate_z_made, j + 1)
                    act.sem_inc(psum_free[(g + j) % 2], 1)

            def retention(h, weave):
                def step(ins):
                    ins.then_inc(ret_act, 1)

                def after(s, steps, name):
                    act.wait_ge(s, at(steps, name, h))
                mixed_in(act, h)
                wait(act, rw_dve, h * (2 * len(RW_DVE)))
                for s in wp_sent:
                    wait(act, s, h * 32)
                after(ret_pe, RET_PE, "v_turned")
                ch.do(act.activation(v_tok[:, :, :], psum[:, 4:6, :], ACT.Copy), wait=False)
                ch.do(act.activation(v_3[:, :], psum[0:3 * NS, 6, :], ACT.Copy), wait=False)
                step(act.activation(v_tok_s[:, :], psum[0:NS, 6, :], ACT.Copy))
                weave("ret_v_turned")
                after(ret_pe, RET_PE, "k_turned")
                act.wait_ge(rc_landed, h * 16 + 16)
                act.wait_ge(rp_sent, h * 32)
                for tt in range(2):
                    ch.do(act.activation(k_tok[:, tt, :], psum[:, 7, tt * 256:(tt + 1) * 256], ACT.Copy,
                                         scale=rc[:, C_KD + tt:C_KD + tt + 1]), wait=False)
                ch.do(act.activation(k_s[:, :], psum[0:3 * NS, 6, 0:256], ACT.Copy, scale=rc[0:3 * NS, C_KD + 2:C_KD + 3]))
                step(act.activation(k_3[:, :], k_s[:, :], ACT.Copy))
                weave("ret_k_turned")
                weave("ret_scores")
                for e in range(2):
                    after(ret_pe, RET_PE, f"kv{e}")
                    step(act.activation(s_out[:, e, :], psum[:, 6 + e, :], ACT.Copy))
                weave("ret_kv1")
                after(ret_pe, RET_PE, "o_prompt")
                step(act.activation(o_T[:, :, 0:SEQ], psum[:, 4:6, :].rearrange("p b (m t) -> p (b m) t", m=2), ACT.Copy))
                weave("ret_o_prompt")
                weave("ret_kv_s3")
                weave("ret_kv_s5")
                after(ret_pe, RET_PE, f"kv_s{SB - 1}o")
                step(act.activation(o_s[:, :], psum[0:NS, 6, :], ACT.Copy))
                weave("ret_o_sample")
                after(ret_dve, RET_DVE, "o_sample_back")
                after(ret_act, RET_ACT, "o_prompt_out")
                step(act.activation(o_sq[:, :, :], o_T[:, :, :], ACT.Square))
                weave("ret_o_sample_turned")
                after(ret_pe, RET_PE, "norm")
                step(act.activation(r_scale[:, :], psum[:, 7, 0:T], ACT.Sqrt, bias=eps_c[:, 0:1], scale=float(D // DV)))
                weave("ret_norm")

            def rwkv(i, q, weave):
                p = i * 2 + q
                pp, rkv = pp2[:, q], rkv2[:, q]
                gap = f"rw{q}_"

                def step(ins):
                    ins.then_inc(rw_act, 1)

                def after(s, steps, name):
                    act.wait_ge(s, at(steps, name, p))
                c = lambda n: pp[:, n:n + 1]
                after(rw_pe, RW_PE, "lora")
                ch.do(act.activation(wag[:, 0, :], psum[:, 4, 0:T], ACT.Sigmoid, bias=c(C_W0)), wait=False)
                step(act.activation(wag[:, 1, :], psum[:, 5, 0:T], ACT.Sigmoid, bias=c(C_A0)))
                act.wait_ge(zs_used, i + 1)
                step(act.activation(ksq[:, :], rkv[:, 1, :], ACT.Square, scale=c(C_KK)))
                weave(gap + "lora")
                after(rw_dve, RW_DVE, "summed")
                ch.do(act.activation(wag[:, 2, :], psum[:, 6, 0:T], ACT.Copy), wait=False)
                ch.do(act.activation(decays[:, 0, :], csum[:, 0, :], ACT.Exp, scale=-KAPPA), wait=False)
                ch.do(act.activation(decays[:, 1, :], csum[:, 0, :], ACT.Exp, scale=KAPPA), wait=False)
                step(act.activation(decays[:, 2, :], csum[:, 1, :], ACT.Exp, scale=-KAPPA))
                weave(gap + "kk_sum")
                after(rw_dve, RW_DVE, "kk_max")
                step(act.activation(kn[:, :], kn[:, :], ACT.Sqrt))
                weave(gap + "kk_root")
                weave(gap + "kk_exps")
                after(rw_pe, RW_PE, "turned")
                ch.do(act.activation(tok[:, :, :, :].rearrange("p a b c -> p a (b c)"), psum[:, 4:6, :], ACT.Copy), wait=False)
                step(act.activation(tok_s[:, :, :].rearrange("p b c -> p (b c)"), psum[0:NS, 6, :], ACT.Copy))
                ch.do(act.activation(xm[:, :, :], ident[:, :].unsqueeze(1).broadcast_to([P, 4, P]), ACT.Copy), wait=False)
                step(act.activation(xm_s[:, :, :], ident[0:NS, 0:NS].unsqueeze(1).broadcast_to([NS, 2, NS]), ACT.Copy))
                for name in ("turned", "prod_k", "prod_s", "x1"):
                    weave(gap + name)
                for s in LEVELS:
                    after(rw_pe, RW_PE, f"y{s}")
                    if s == 2:
                        ch.do(act.activation(ym_s[:, :, :].rearrange("p a b -> p (a b)"), psum[0:NS, 4, 0:2 * NS], ACT.Copy), wait=False)
                    step(act.activation(ym[:, :, :].rearrange("p a b -> p (a b)"), psum[:, 5, :], ACT.Copy))
                    weave(gap + f"y{s}")
                    weave(gap + f"d{s}")
                after(rw_pe, RW_PE, "nv")
                ch.do(act.activation(nv[:, 0:2, :].rearrange("p a b -> p (a b)"), psum[:, 4, 0:256], ACT.Copy), wait=False)
                step(act.activation(nv[0:NS, 2, :], psum[0:NS, 4, 256:384], ACT.Copy))
                weave(gap + "nv")
                after(rw_pe, RW_PE, "gh")
                ch.do(act.activation(hT[:, :, :].rearrange("p a b -> p (a b)"), psum[:, 6, 0:256], ACT.Copy), wait=False)
                ch.do(act.activation(hr[:, 1, :], ar[:, 1, SEQ:T], ACT.Copy), wait=False)
                step(act.activation(hr[:, 0, :], psum[:, 6, 256:256 + NS], ACT.Copy))
                for name in ("gh", "upd0", "u1", "upd1", "u2", "upd2", "u3", "upd3"):
                    weave(gap + name)
                after(rw_pe, RW_PE, "u_s")
                step(act.activation(us[:, :, :].rearrange("p a (b t) -> p b a t", t=ST),
                                    psum[:, 5, 0:64].rearrange("p (b a t) -> p b a t", a=2, t=ST), ACT.Copy))
                weave(gap + "u_s")
                weave(gap + "u_s_turned")
                after(rw_pe, RW_PE, "out")
                step(act.activation(ysb[:, 0:SEQ], psum[:, 7, 0:SEQ], ACT.Copy))
                weave(gap + "out")
                after(rw_dve, RW_DVE, "centred")
                step(act.activation(ksq[:, :], yc[:, :], ACT.Square))
                weave(gap + "mean")
                after(rw_pe, RW_PE, "var")
                step(act.activation(y_rms[:, :], psum[:, 4, 0:T], ACT.Sqrt, bias=eps_c[:, 1:2]))
                weave(gap + "var")

            def units_of(i, weave):
                retention(i, weave)
                act.wait_ge(ret_dve, at(RET_DVE, "done", i))
                units_free_of_retention(act, i)
                for q in range(2):
                    rwkv(i, q, weave)

            for n in range(MIX_BLOCKS):
                for q in range(4):
                    if n or q:
                        quarter(0, mix_ph, n, q)

            def with_projections(i):
                def mine(n, q):
                    if (n, q) == (last_block(0), 3):
                        act.wait_ge(zs_used, i + 1)
                    quarter(i, next_ph, n, q)
                units_of(i, Weave(MIX_BLOCKS, mine))
            ch.loop(RH - 1, with_projections)
            units_of(RH - 1, Weave(GATE_BLOCKS, gates_quarter))

            split(0, ret_o_ph[0] + 1)
            mixing_over(act)
            for k in range(RH * VT):
                act.activation(or_hi[:, k, :], o_ret[:, k, :], ACT.Copy).then_inc(o_hi, 1)

            def ret_o(i):
                for j in range(4):
                    if j >= 2 or not is_first(i):
                        split(i * 4, ret_o_ph[0] + j)
                if is_first(i):
                    for k in range(PAIRS):
                        act.activation(ow_hi[:, k, :], o_rw[:, k, :], ACT.Copy).then_inc(o_hi, 1)
            loop(act, PAIRS // 2, ret_o)

            def hi_part(i, j):
                act.wait_ge(merged, i * 2 + (j + 1))
                act.activation(m_hi[:, bass.ds(i * 4 + 2 * j, 2), :], prod_m[:, :, :], ACT.Copy).then_inc(merged_hi, 1)

            def rw_o(i):
                split(i * 2, rw_o_ph[0])
                if not is_first(i):
                    hi_part(i - 1, 1)
                split(i * 2, rw_o_ph[0] + 1)
                hi_part(i, 0)
            loop(act, PAIRS // 2, rw_o)
            split(0, w_out_ph[0])
            hi_part(PAIRS // 2 - 1, 1)

            def out(i):
                for j in range(4):
                    if j or not is_first(i):
                        split(i * 4, w_out_ph[0] + j)
            loop(act, 4, out)
            feed(1)
            norm(3)

        @block.vector
        def _(dve):
            ch = Chain(dve, dve_chain)
            do = ch.do

            def split_half(n, first, half):
                slot, c = first % 2, slice(half * BLK // 2, (half + 1) * BLK // 2)
                dve.wait_ge(hi_made, n + (first + 1))
                ins = dve.tensor_tensor(w_lo[:, slot, c], raw[:, slot, c], w_hi[:, slot, c].bitcast(F32), ALU.subtract)
                if half:
                    ins.then_inc(lo_made, 1)

            def split(n, first, cols=BLK):
                slot = first % 2
                dve.wait_ge(hi_made, n + (first + 1))
                dve.tensor_tensor(w_lo[:, slot, 0:cols], raw[:, slot, 0:cols], w_hi[:, slot, 0:cols].bitcast(F32),
                                  ALU.subtract).then_inc(lo_made, 1)

            def norm(r, first=None):
                if first is not None:
                    split(0, first)
                dve.wait_ge(root_made, r + 1)
                do(dve.reciprocal(scale[:, :], scale[:, :]))

                def tile(k):
                    out = x[:, k, :] if r == 3 else prod[:, k % 2, :]
                    dve.scalar_tensor_tensor(out=out, in0=x[:, k, :], scalar=gains[:, r, k:k + 1], in1=scale[:, :],
                                             op0=ALU.mult, op1=ALU.mult).then_inc(normed, 1)
                tile(0)
                for k in range(KT):
                    if k + 1 < KT:
                        if k >= 1 and r < 3:
                            dve.wait_ge(normed_lo, r * KT + k)
                        tile(k + 1)
                    if r < 3:
                        dve.wait_ge(normed_hi, r * KT + k + 1)
                        dve.tensor_tensor(h_lo[:, k, :], prod[:, k % 2, :], h_hi[:, k, :].bitcast(F32),
                                          ALU.subtract).then_inc(normed_lo, 1)
                    if k == 5 and first is not None:
                        split(0, first + 1)

            do(dve.memset(eps_c[:, 0:1], EPS), wait=False)
            do(dve.memset(eps_c[:, 1:2], GN_EPS))
            dve.sem_inc(eps_made, 1)

            def sum_squares(pr):
                do(dve.tensor_tensor(sq[:, :, :], x[:, pr, :], x[:, pr, :], ALU.mult))
                do(dve.tensor_tensor(sum_sq[:, :, :], sum_sq[:, :, :], sq[:, :, :], ALU.add))
            do(dve.memset(sum_sq[:, :, :], 0.0))
            for k in range(0, KT, 2):
                if k % 4 == 0:
                    dve.wait_ge(x_landed[k // 4], 16)
                sum_squares(slice(k, k + 2))
            dve.sem_inc(squares, 1)
            dve.wait_ge(loaded, 16 * LOADS)

            def feed(n):
                norm(2 * n, ffn[n][0][0][0])
                for f in range(2):
                    (b, g), (bd, gd) = ffn[n][f]
                    done = (2 * n + f) * (HT // 2)
                    gates = done

                    def product(i):
                        dve.wait_ge(used, i * 4 + (b + 4))
                        dve.wait_ge(gate_made, i + (gates + 1))
                        wait(dve, hidden_lo, i + done)
                        s = 2 * ((g + 1) % 2)
                        dve.tensor_tensor(prod[:, :, :], psum[:, s:s + 2, 0:T], gate[:, :, :], ALU.mult).then_inc(hidden, 1)
                        dve.wait_ge(hidden, i + (done + 1))
                        dve.sem_inc(psum_free[(g + 1) % 2], 1)

                    def low(i):
                        dve.wait_ge(hidden_hi, i + (done + 1))
                        pr = bass.ds(i * 2, 2)
                        dve.tensor_tensor(g_lo[:, pr, :], prod[:, :, :], g_hi[:, pr, :].bitcast(F32),
                                          ALU.subtract).then_inc(hidden_lo, 1)

                    def up(i):
                        if not is_first(i):
                            split(i * 4, b)
                        if not is_first(i):
                            product(i - 1)
                        if f or not is_first(i):
                            split(i * 4, b + 1)
                        if not is_first(i):
                            low(i - 1)
                        split(i * 4, b + 2)
                        split(i * 4, b + 3)
                    loop(dve, HT // 2, up)
                    split(0, bd, DOWN)
                    product(HT // 2 - 1)
                    low(HT // 2 - 1)
                    add(4, 8, bd, gd, DOWN, 0.5, f == 1, following=ffn[n][1][0][0] if f == 0 else None)

            def add(times, per, b, g, cols, factor, final, following=None):
                def take(i, j):
                    dve.wait_ge(used, i * per + (b + (j + 1) * per // 2))
                    s = 2 * ((g + j) % 2)
                    pr = bass.ds(i * 4 + 2 * j, 2)
                    do(dve.scalar_tensor_tensor(out=x[:, pr, :], in0=psum[:, s:s + 2, 0:T], scalar=factor, in1=x[:, pr, :],
                                                op0=ALU.mult, op1=ALU.add))
                    dve.sem_inc(psum_free[(g + j) % 2], 1)
                    if final:
                        sum_squares(pr)

                def body(i):
                    for j in range(per):
                        if j or not is_first(i):
                            split(i * per, b + j, cols)
                        if j == 0 and not is_first(i):
                            take(i - 1, 1)
                        if j == per // 2:
                            take(i, 0)
                if final:
                    do(dve.memset(sum_sq[:, :, :], 0.0))
                ch.loop(times, body, 6 if final else 2)
                if following is not None:
                    split(0, following)
                take(times - 1, 1)
                if final:
                    dve.sem_inc(squares, 1)

            feed(0)
            b, g = lora_ph
            norm(1, b)
            split(0, b + 2, LORA2)
            split(0, mix_ph[0])
            split(0, mix_ph[0] + 1)
            dve.wait_ge(mix_loaded, 16 * MIX_LOADS)
            do(dve.memset(zs[:, :, :, 0:1], 0.0), wait=False)
            do(dve.memset(last[:, :, :], 0.0), wait=False)
            def samples(v):
                return v.rearrange("p (b t) -> p b t", t=ST + 1)

            def shift(out, tmp, z, mu):
                do(dve.tensor_tensor(tmp[:, 0:SEQ], z[:, 0:SEQ], z[:, 1:1 + SEQ], ALU.subtract), wait=False)
                zq = samples(z[:, 1 + SEQ:])
                tq, oq = (v[:, SEQ:T].rearrange("p (b t) -> p b t", t=ST) for v in (tmp, out))
                do(dve.tensor_tensor(tq, zq[:, :, 0:ST], zq[:, :, 1:], ALU.subtract))
                do(dve.scalar_tensor_tensor(out=out[:, 0:SEQ], in0=tmp[:, 0:SEQ], scalar=mu, in1=z[:, 1:1 + SEQ],
                                            op0=ALU.mult, op1=ALU.add), wait=False)
                do(dve.scalar_tensor_tensor(out=oq, in0=tq, scalar=mu, in1=zq[:, :, 1:], op0=ALU.mult, op1=ALU.add))

            for s in range(2):
                dve.wait_ge(psum_free[s], g // 2 + 1)
            for k in range(3):
                w = P if k < 2 else GATE1
                z = zs[0:w, k // 2, k % 2, :]
                do(dve.tensor_copy(samples(z[:, 1 + SEQ:])[:, :, 0], lpk[0:w, k * SB:(k + 1) * SB]))
                shift(rkv[0:w, k, :], rot[0:w, k % 2, :], z, lpk[0:w, 3 * SB + k:3 * SB + k + 1])
                do(dve.tensor_copy(last[0:w, k, 0:1], z[:, SEQ:SEQ + 1]), wait=False)
                do(dve.tensor_copy(last[0:w, k, 1:], samples(z[:, 1 + SEQ:])[:, :, ST]))
            dve.sem_inc(lora_shifted, 1)
            dve.sem_inc(last_made, 1)

            def rotate(i, ph, j):
                b, g = ph
                dve.wait_ge(used, i * MIX_BLOCKS + (b + last_block(j) + 1))
                s = 2 * ((g + j) % 2)
                factor = 1.0 if j == 3 else DK ** -0.5

                def times(n, bank, t):
                    do(dve.scalar_tensor_tensor(out=rot[:, n, :], in0=psum[:, bank, 0:T], scalar=factor,
                                                in1=trig[:, t, :], op0=ALU.mult, op1=ALU.mult), wait=(n == 1))
                times(0, s, 0)
                times(1, s + 1, 1)
                do(dve.tensor_tensor(qk[:, 2 * (j - 3), :], rot[:, 0, :], rot[:, 1, :], ALU.subtract))
                times(0, s, 1)
                times(1, s + 1, 0)
                dve.sem_inc(psum_free[(g + j) % 2], 1)
                do(dve.tensor_tensor(qk[:, 2 * (j - 3) + 1, :], rot[:, 0, :], rot[:, 1, :], ALU.add))

            def quarter(i, ph, n, q):
                if q in (0, 2):
                    split_half(i * MIX_BLOCKS, ph[0] + n + 1, q // 2)
                if q == 3 and n in (last_block(3), last_block(4)):
                    rotate(i, ph, 3 if n == last_block(3) else 4)

            def shifts(i):
                mixed_in(dve, i)
                for q in range(2):
                    dve.wait_ge(pp_landed[q], i * 32 + 32)
                    for a in range(3):
                        z = zs[:, a, q, :]
                        do(dve.tensor_copy(samples(z[:, 1 + SEQ:])[:, :, 0], pp2[:, q, C_SHIFT + a * SB:C_SHIFT + (a + 1) * SB]))
                        shift(rkv2[:, q, a, :], rot[:, a % 2, :], z, pp2[:, q, C_MU + a:C_MU + a + 1])
                dve.wait_ge(last_sent, i * 16 + 16)
                for a in range(3):
                    for q in range(2):
                        z = zs[:, a, q, :]
                        do(dve.tensor_copy(last[:, 2 * a + q, 0:1], z[:, SEQ:SEQ + 1]), wait=False)
                        do(dve.tensor_copy(last[:, 2 * a + q, 1:], samples(z[:, 1 + SEQ:])[:, :, ST]), wait=(a + q == 3))
                dve.sem_inc(zs_used, 1)
                dve.sem_inc(last_made, 1)

            def retention(h, weave):
                def after(s, steps, name):
                    dve.wait_ge(s, at(steps, name, h))

                def step(ins):
                    ins.then_inc(ret_dve, 1)
                for s in wp_sent:
                    wait(dve, s, h * 32)
                mixed_in(dve, h)
                after(ret_act, RET_ACT, "v_out")
                step(dve.tensor_tensor(v_3[NS:2 * NS, :], psum[NS:2 * NS, 6, :], v_3[NS:2 * NS, :].bitcast(F32), ALU.subtract))
                dve.wait_ge(rc_landed, h * 16 + 16)
                decay = rc[:, C_QD:C_KD].rearrange("p (b t) -> p b t", t=NS)
                for e in range(2):
                    ins = dve.tensor_tensor(q_own[:, e, :, :], qk[:, e, SEQ:T].unsqueeze(1).broadcast_to([P, SB, NS]),
                                            decay, ALU.mult)
                    step(ins) if e else do(ins, wait=False)
                weave("ret_v_turned")
                weave("ret_k_turned")
                after(ret_pe, RET_PE, "scores")
                do(dve.tensor_tensor(scores[:, 0:SEQ], psum[:, 4, 0:SEQ], rc[:, 0:SEQ], ALU.mult), wait=False)
                do(dve.tensor_tensor(scores[:, SEQ:384], psum[:, 5, 0:P], rc[:, 0:P], ALU.mult), wait=False)
                step(dve.tensor_tensor(scores[0:NS, 384:384 + NS], psum[0:NS, 5, P:P + NS], rc[0:NS, 384:384 + NS], ALU.mult))
                weave("ret_scores")
                after(ret_act, RET_ACT, "k_out")
                rest = slice(2 * NS, 3 * NS)
                step(dve.tensor_tensor(k_3[rest, :], k_s[rest, :], k_3[rest, :].bitcast(F32), ALU.subtract))
                after(ret_dve, RET_DVE, "k_parts")
                step(dve.tensor_tensor(k_own[:, :, :], k_3[:, :].bitcast(F32).unsqueeze(1).broadcast_to([3 * NS, SB, DK]),
                                       own[:, :].unsqueeze(2).broadcast_to([3 * NS, SB, DK]), ALU.mult))
                weave("ret_kv1")
                shifts(h)
                weave("ret_o_prompt")
                for bb in range(SB):
                    for n, e in enumerate("eo"):
                        after(ret_pe, RET_PE, f"kv_s{bb}{e}")
                        bank = (7, 4, 5)[(2 * bb + n) % 3]
                        dve.scalar_tensor_tensor(out=s_ret[:, bb % SLOTS, n, :], in0=s_ret[:, bb % SLOTS, n, :],
                                                 scalar=rc[:, C_KD + 3:C_KD + 4], in1=psum[:, bank, :], op0=ALU.mult,
                                                 op1=ALU.add).then_inc(s_new, 1)
                    if bb in (3, 5):
                        weave(f"ret_kv_s{bb}")
                weave("ret_o_sample")
                after(ret_pe, RET_PE, "o_sample_turned")
                step(dve.tensor_copy(o_T[:, :, SEQ:T], psum[:, 6, 0:VT * NS].rearrange("p (m t) -> p m t", m=VT)))
                weave("ret_o_sample_turned")
                after(ret_act, RET_ACT, "squared")
                do(dve.tensor_tensor(o_T[:, :, :], o_T[:, :, :], vg[:, 1, :, :], ALU.mult), wait=False)
                after(ret_act, RET_ACT, "root")
                do(dve.reciprocal(r_scale[:, :], r_scale[:, :]))
                step(dve.tensor_tensor(o_ret[:, bass.ds(h * VT, VT), :], o_T[:, :, :],
                                       r_scale[:, :].unsqueeze(1).broadcast_to([P, VT, T]), ALU.mult))
                after(ret_dve, RET_DVE, "done")
                weave("ret_norm")

            def rwkv(i, q, weave):
                p = i * 2 + q
                pp, rkv, s0 = pp2[:, q], rkv2[:, q], s0_2[:, q]
                gap = f"rw{q}_"

                def after(s, steps, name):
                    dve.wait_ge(s, at(steps, name, p))

                def step(ins):
                    ins.then_inc(rw_dve, 1)

                def c(n):
                    return pp[:, n:n + 1]

                def mul(out, a, b, wait=True):
                    do(dve.tensor_tensor(out, a, b, ALU.mult), wait=wait)
                r_, k_, v_ = (rkv[:, n, :] for n in range(3))
                do(dve.tensor_scalar(c(C_OKA), c(C_KA), -1.0, 1.0, ALU.mult, ALU.add), wait=False)
                after(rw_act, RW_ACT, "gates")
                do(dve.tensor_tensor_scan(csum[:, 0, :], run_m[:, :], wag[:, 0, :], 0.0, ALU.mult, ALU.add))
                step(dve.tensor_tensor(csum[:, 1, :], csum[:, 0, :], wag[:, 0, :], ALU.subtract))
                weave(gap + "lora")
                after(rw_pe, RW_PE, "kk_sum")
                after(rw_dve, RW_DVE, "summed")
                step(dve.tensor_scalar(kn[:, :], psum[:, 7, 0:T], float(N), 1e-24, ALU.mult, ALU.max))
                do(dve.tensor_scalar(k2[:, :], wag[:, 1, :], c(C_KA), c(C_OKA), ALU.mult, ALU.add))
                mul(k2[:, :], k_, k2[:, :], wait=False)
                weave(gap + "kk_sum")
                after(rw_act, RW_ACT, "exps")
                mul(bc[:, :], wag[:, 1, :], decays[:, 1, :], wait=False)
                mul(ar[:, 1, :], r_, decays[:, 0, :])
                mul(kc[:, :], k2[:, :], decays[:, 1, :])
                step(dve.scalar_tensor_tensor(out=rk[:, :], in0=k2[:, :], scalar=c(C_RK), in1=r_, op0=ALU.mult, op1=ALU.mult))
                weave(gap + "kk_root")
                after(rw_act, RW_ACT, "root")
                do(dve.reciprocal(kn[:, :], kn[:, :]))
                do(dve.scalar_tensor_tensor(out=kk[:, :], in0=k_, scalar=c(C_KK), in1=kn[:, :], op0=ALU.mult, op1=ALU.mult))
                do(dve.scalar_tensor_tensor(out=ar[:, 0, :], in0=kk[:, :], scalar=-1.0, in1=decays[:, 2, :],
                                            op0=ALU.mult, op1=ALU.mult), wait=False)
                step(dve.tensor_tensor(bc[:, :], bc[:, :], kk[:, :], ALU.mult))
                weave(gap + "kk_exps")
                after(rw_pe, RW_PE, "bonus")
                step(dve.scalar_tensor_tensor(out=bonus[:, :], in0=psum[:, 7, 0:T], scalar=float(N), in1=v_,
                                              op0=ALU.mult, op1=ALU.mult))
                weave(gap + "turned")
                for n, (name, x1, x2) in enumerate((("b", mt, pt), ("k", nt, qt))):
                    after(rw_pe, RW_PE, f"prod_{name}")
                    for hd in range(2):
                        src = psum[:, 4 + 2 * n + hd, :].rearrange("p (t a i) -> p t a i", t=2, a=2)
                        for a, dst in enumerate((x1, x2)):
                            ins = dve.tensor_tensor(dst[:, 2 * hd:2 * hd + 2, :], src[:, :, a, :],
                                                    tri[:, a, :].unsqueeze(1).broadcast_to([P, 2, P]), ALU.mult)
                            if hd == 1 and a == 1:
                                step(ins)
                            else:
                                do(ins, wait=False)
                weave(gap + "prod_k")
                after(rw_pe, RW_PE, "prod_s")
                tri2 = tri_s[:, :, :].rearrange("p a i -> p (a i)").unsqueeze(1).broadcast_to([NS, 2, 2 * NS])
                for hd in range(2):
                    ins = dve.tensor_tensor(ms[:, 2 * hd:2 * hd + 2, :, :].rearrange("p a b i -> p a (b i)"),
                                            psum[0:NS, 4 + hd, 0:4 * NS].rearrange("p (a b) -> p a b", a=2), tri2, ALU.mult)
                    step(ins) if hd else do(ins, wait=False)
                weave(gap + "prod_s")
                after(rw_pool, RW_POOL, "lm_s1")
                do(dve.tensor_tensor(xt[:, :, :], lm[:, :, :], ident[:, :].unsqueeze(1).broadcast_to([P, 4, P]), ALU.add), wait=False)
                do(dve.tensor_tensor(xt_s[:, :, :], lm_s[:, :, :], ident[0:NS, 0:NS].unsqueeze(1).broadcast_to([NS, 2, NS]),
                                     ALU.add), wait=False)
                after(rw_pe, RW_PE, "x1")
                ev = xm_s[:, :, :].rearrange("p q (b two) -> p q b two", two=2)[:, :, :, 0]
                do(dve.tensor_tensor(ev, ev, psum[0:NS, 5, 256:288].rearrange("p (q b) -> p q b", q=2), ALU.add), wait=False)
                ev = xm[:, :, :].rearrange("p q (b two) -> p q b two", two=2)[:, :, :, 0]
                step(dve.tensor_tensor(ev, ev, psum[:, 5, 0:256].rearrange("p (q b) -> p q b", q=4), ALU.add))
                weave(gap + "x1")
                for s in LEVELS:
                    weave(gap + f"y{s}")
                    after(rw_pe, RW_PE, f"d{s}")
                    if s == 2:
                        x2 = xt_s[:, :, :].rearrange("p q (b two s) -> p q b two s", two=2, s=s)
                        for hd in range(2):
                            do(dve.tensor_tensor(x2[:, hd, :, 1], x2[:, hd, :, 1],
                                                 psum[0:NS, 7, 256 + 16 * hd:272 + 16 * hd].rearrange("p (b s) -> p b s", s=s),
                                                 ALU.add), wait=False)
                    if s < 32:
                        x2 = xm[:, :, :].rearrange("p q (b two s) -> p q b two s", two=2, s=s)[:, :, :, 0]
                        do(dve.tensor_tensor(x2, x2, psum[:, 6, 0:256].rearrange("p (q b s) -> p q b s", q=4, s=s), ALU.add),
                           wait=False)
                    x2 = xt[:, :, :].rearrange("p q (b two s) -> p q b two s", two=2, s=s)[:, :, :, 1]
                    step(dve.tensor_tensor(x2, x2, psum[:, 7, 0:256].rearrange("p (q b s) -> p q b s", q=4, s=s), ALU.add))
                    after(rw_dve, RW_DVE, f"x{s}")
                    weave(gap + f"d{s}")
                weave(gap + "nv")
                after(rw_pe, RW_PE, "gh")
                do(dve.tensor_copy(gm[0:NS, 2, :], psum[0:NS, 5, 256:384]), wait=False)
                do(dve.tensor_copy(um[0:CH, 0, :], psum[0:CH, 5, 0:P]), wait=False)
                step(dve.tensor_copy(gm[:, 0:2, :].rearrange("p a b -> p (a b)"), psum[:, 5, 0:256]))
                weave(gap + "gh")
                if q:
                    dve.wait_ge(wp_sent[0], i * 32 + 32)
                for n in range(1, 5):
                    after(rw_pe, RW_PE, f"upd{n - 1}")
                    if n == 1:
                        do(dve.tensor_copy(stt[:, :], psum[:, 7, 0:P]))
                    else:
                        do(dve.tensor_tensor(stt[:, :], psum[:, 7, 0:P], st[:, n - 2, :], ALU.add))
                    step(dve.scalar_tensor_tensor(out=st[:, n - 1, :], in0=stt[:, :], scalar=decays[:, 0, n * CH - 1:n * CH],
                                                  in1=blocks_m[:, :], op0=ALU.mult, op1=ALU.mult))
                    after(rw_dve, RW_DVE, f"s{n}")
                    weave(gap + f"upd{n - 1}")
                    if n < 4:
                        tt, off = divmod(n * CH, P)
                        rr = slice(off, off + CH)
                        after(rw_pe, RW_PE, f"u{n}")
                        step(dve.tensor_tensor(um[rr, tt, :], psum[rr, 4, 0:P], gm[rr, tt, :], ALU.add))
                        weave(gap + f"u{n}")
                weave(gap + "u_s")
                after(rw_pe, RW_PE, "u_s_turned")
                step(dve.tensor_tensor(um_s[:, :], psum[0:NS, 6, 0:P], gm[0:NS, 2, :], ALU.add))
                weave(gap + "u_s_turned")
                after(rw_pe, RW_PE, "upd_s")
                for hd in range(2):
                    v = slice(64 * hd, 64 * hd + 64)
                    do(dve.tensor_tensor(s0[v, :, :], s0[v, :, :],
                                         psum[v, 4:6, :].rearrange("p q (b c) -> p (q b) c", b=4)[:, :, v], ALU.add),
                       wait=(hd == 1))
                end = decays[:, 0, SEQ:T].rearrange("p (b t) -> p b t", t=ST)[:, :, ST - 1]
                step(dve.tensor_tensor(s0[:, :, :], s0[:, :, :], end.unsqueeze(2).broadcast_to([P, SB, N]), ALU.mult))
                after(rw_act, RW_ACT, "y_prompt_out")
                step(dve.tensor_tensor(ysb[:, SEQ:T], psum[:, 7, SEQ:T], us[:, 1, :], ALU.add))
                weave(gap + "out")
                after(rw_pe, RW_PE, "mean")
                step(dve.tensor_tensor(yc[:, :], ysb[:, :], psum[:, 6, 0:T], ALU.subtract))
                weave(gap + "mean")
                after(rw_act, RW_ACT, "y_root")
                do(dve.reciprocal(y_rms[:, :], y_rms[:, :]))
                weave(gap + "var")
                do(dve.scalar_tensor_tensor(out=yc[:, :], in0=yc[:, :], scalar=c(C_LNW), in1=y_rms[:, :],
                                            op0=ALU.mult, op1=ALU.mult))
                do(dve.scalar_tensor_tensor(out=yc[:, :], in0=yc[:, :], scalar=c(C_LNB), in1=bonus[:, :],
                                            op0=ALU.add, op1=ALU.add))
                step(dve.tensor_tensor(o_rw[:, bass.ds(p, 1), :].rearrange("p a t -> p (a t)"), yc[:, :], wag[:, 2, :], ALU.mult))
                after(rw_dve, RW_DVE, "done")

            def units_of(i, weave):
                retention(i, weave)
                units_free_of_retention(dve, i)
                for q in range(2):
                    rwkv(i, q, weave)

            for n in range(MIX_BLOCKS):
                for q in range(4):
                    if n or q not in (0, 2):
                        quarter(0, mix_ph, n, q)

            def gates_quarter(n, q):
                if q in (0, 2):
                    split_half(0, gates_ph[0] + n + 1, q // 2)
            dve.wait_ge(spilled, 16)
            ch.loop(RH - 1, lambda i: units_of(i, Weave(MIX_BLOCKS, lambda n, q: quarter(i, next_ph, n, q))))
            units_of(RH - 1, Weave(GATE_BLOCKS, gates_quarter))

            split(0, ret_o_ph[0] + 1)
            mixing_over(dve)
            for k in range(RH * VT):
                dve.wait_ge(o_hi, k + 1)
                dve.tensor_tensor(or_lo[:, k, :], o_ret[:, k, :], or_hi[:, k, :].bitcast(F32), ALU.subtract).then_inc(o_lo, 1)

            def product(i, j, n):
                b, g, per = (*ret_o_ph, 2) if n == 0 else (*rw_o_ph, 1)
                s = 2 * ((g + j) % 2)
                dve.wait_ge(used, i * (2 * per) + (b + (j + 1) * per))
                dve.wait_ge(gate_back[j], i * 16 + 16 * (n * PAIRS // 2 + 1))
                pr = bass.ds(i * 4 + 2 * j, 2)
                if n == 0:
                    ins = dve.tensor_tensor(part[:, pr, :], psum[:, s:s + 2, 0:T], gate_m[:, j, :, :], ALU.mult)
                else:
                    wait(dve, merged_lo, i * 2 + j)
                    ins = dve.tensor_tensor(prod_m[:, :, :], psum[:, s:s + 2, 0:T], gate_m[:, j, :, :], ALU.mult)
                ins.then_inc(gate_used, 1)
                dve.wait_ge(gate_used, i * 2 + (n * PAIRS + j + 1))
                dve.sem_inc(psum_free[(g + j) % 2], 1)
                if n:
                    dve.tensor_tensor(prod_m[:, :, :], prod_m[:, :, :], part[:, pr, :], ALU.add).then_inc(merged, 1)
                    dve.wait_ge(merged_hi, i * 2 + (j + 1))
                    dve.tensor_tensor(m_lo[:, pr, :], prod_m[:, :, :], m_hi[:, pr, :].bitcast(F32),
                                      ALU.subtract).then_inc(merged_lo, 1)

            def ret_o(i):
                if not is_first(i):
                    split(i * 4, ret_o_ph[0])
                    product(i - 1, 1, 0)
                    split(i * 4, ret_o_ph[0] + 1)
                split(i * 4, ret_o_ph[0] + 2)
                product(i, 0, 0)
                split(i * 4, ret_o_ph[0] + 3)
                if is_first(i):
                    for k in range(PAIRS):
                        dve.wait_ge(o_hi, RH * VT + k + 1)
                        dve.tensor_tensor(ow_lo[:, k, :], o_rw[:, k, :], ow_hi[:, k, :].bitcast(F32), ALU.subtract).then_inc(o_lo, 1)
            loop(dve, PAIRS // 2, ret_o)

            def rw_o(i):
                split(i * 2, rw_o_ph[0])
                if is_first(i):
                    product(PAIRS // 2 - 1, 1, 0)
                else:
                    product(i - 1, 1, 1)
                split(i * 2, rw_o_ph[0] + 1)
                product(i, 0, 1)
            loop(dve, PAIRS // 2, rw_o)
            split(0, w_out_ph[0])
            product(PAIRS // 2 - 1, 1, 1)
            dve.wait_ge(x_back, 16)
            add(4, 4, *w_out_ph, BLK, 1.0, True)
            feed(1)
            norm(3)

        @block.gpsimd
        def _(pool):
            for n in range(4):
                pool.dma_start(x[:, 4 * n:4 * n + 4, :], d["x"][:, 4 * n:4 * n + 4, :]).then_inc(x_landed[n], 16)
            for dst, src in ((mean_w, "mean_w"), (head_w, "head_w"), (ident, "ident"), (gains, "gains")):
                pool.dma_start(dst[:], d[src]).then_inc(loaded, 16)
            pool.wait_ge(used, lora_ph[0])
            for dst, src in ((lpk, "lpk"), (trig, "trig"), (levels_m, "levels_m"), (tri, "tri"), (tri_s, "tri_s"), (own, "own"),
                             (blocks_m, "blocks_m"), (run_m, "run_m")):
                pool.dma_start(dst[:], d[src]).then_inc(mix_loaded, 16)
            pool.wait_ge(normed_lo, 2 * KT)
            pool.dma_start(d["spill"], x[:, :, :]).then_inc(spilled, 16)
            pool.wait_ge(last_made, 1)
            pool.dma_start(d["last_lora"], last[:, 0:3, :]).then_inc(last_sent, 16)
            pool.wait_ge(mix_loaded, 16 * MIX_LOADS)
            pool.wait_ge(lora_made, 1)

            def move(dst, src, done):
                pool.sem_inc(parted, 1)
                pool.dma_start(dst, src).then_inc(done, 16)

            def bring_pair(i, q, p):
                move(pp2[:, q, :], d["pp"][p], pp_landed[q])
                move(s0_2[:, q, :, :], d["s0"][p], pp_landed[q])

            def mix_step(i, final=False):
                if not is_first(i):
                    pool.wait_ge(rw_dve, i * (2 * len(RW_DVE)))
                    for s in wp_sent:
                        pool.wait_ge(s, i * 32)
                move(rc[:, :], d["rc"][i], rc_landed)
                per = 16 * (SB // SLOTS)

                def bring(bb):
                    s = bb % SLOTS
                    wait(pool, s_sent[s], i * per + 16 * (bb // SLOTS))
                    move(s_ret[:, s, :, :], d["s_ret"][i, bb], s_landed[s])
                for bb in range(SLOTS):
                    bring(bb)
                pool.wait_ge(last_made, i + 2)
                move(d["last"][i], last[:, :, :], last_sent)
                for e in range(2):
                    pool.wait_ge(ret_act, at(RET_ACT, f"state{e}", i))
                    move(d["ret_p"][i, e], s_out[:, e, :], rp_sent)
                for bb in range(SB):
                    pool.wait_ge(s_new, i * (2 * SB) + 2 * bb + 2)
                    move(d["ret_s"][i, bb], s_ret[:, bb % SLOTS, :, :], s_sent[bb % SLOTS])
                    if 1 <= bb <= SLOTS:
                        bring(bb - 1 + SLOTS)
                pool.wait_ge(ret_dve, at(RET_DVE, "done", i))
                units_free_of_retention(pool, i)
                for q in range(2):
                    p = i * 2 + q
                    for n, s in enumerate((1,) + LEVELS):
                        if s == 1:
                            pool.wait_ge(rw_dve, at(RW_DVE, "masked_b", p))
                        elif s == 2:
                            pool.wait_ge(rw_dve, at(RW_DVE, "x1", p))
                        else:
                            pool.wait_ge(rw_pe, at(RW_PE, f"y{s // 2}", p))
                        pool.tensor_tensor(lm[:, :, :], mt[:, :, :], levels_m[:, n, :].unsqueeze(1).broadcast_to([P, 4, P]),
                                           ALU.mult).then_inc(rw_pool, 1)
                        if s == 1:
                            pool.wait_ge(rw_dve, at(RW_DVE, "masked_s", p))
                        if s <= 2:
                            pool.tensor_tensor(lm_s[:, :, :], ms[:, :, 0, :].rearrange("p (h n) i -> p h n i", n=2)[:, :, 0, :],
                                               levels_m[0:NS, n, 0:NS].unsqueeze(1).broadcast_to([NS, 2, NS]),
                                               ALU.mult).then_inc(rw_pool, 1)
                    own_b = own[0:NS, :].unsqueeze(2).broadcast_to([NS, SB, P])
                    for n, name in ((2, f"y{LEVELS[-1]}"), (1, "nv")):
                        pool.wait_ge(rw_pe, at(RW_PE, name, p))
                        pool.tensor_tensor((b_own, k_own_s)[n - 1][:, :, :], tok_s[:, n, :].unsqueeze(1).broadcast_to([NS, SB, P]),
                                           own_b, ALU.mult).then_inc(rw_pool, 1)
                    pool.wait_ge(rw_dve, at(RW_DVE, "s4", p))
                    for hd in range(2):
                        v = slice(64 * hd, 64 * hd + 64)
                        move(d["rwkv_p"][p, v, :], st[v, 3, v], wp_sent[q])
                    pool.wait_ge(rw_dve, at(RW_DVE, "s_s", p))
                    move(d["rwkv_s"][p], s0_2[:, q, :, :], ws_sent[q])
                    if not final:
                        pool.wait_ge(rw_dve, at(RW_DVE, "done", p))
                        pool.wait_ge(ws_sent[q], i * 16 + 16)
                        bring_pair(i + 1, q, i * 2 + (q + 2))
            for q in range(2):
                bring_pair(0, q, q)
            loop(pool, RH - 1, mix_step)
            mix_step(RH - 1, True)
            mixing_over(pool)
            pool.wait_ge(spilled, 16)
            pool.wait_ge(o_lo, RH * VT)
            pool.dma_start(x[:, :, :], d["spill"]).then_inc(x_back, 16)


def consts():
    f = np.float32
    i = np.arange(P)
    j, i = np.meshgrid(i, i, indexing="ij")
    same = (j // CH == i // CH)
    tri = np.stack([same & (j < i), same & (j <= i)], 1)
    lev = np.stack([(j // (2 * s) == i // (2 * s)) & (j % (2 * s) < s) & (i % (2 * s) >= s)
                    for s in (1,) + LEVELS], 1)
    js, is_ = j[:NS, :NS], i[:NS, :NS]
    mine = js // ST == is_ // ST
    run = np.ones(T)
    run[:SEQ:CH] = 0
    run[SEQ::ST] = 0
    half = DK // 2
    inv = (f(1.0) / (f(10000.0) ** np.linspace(0.0, 1.0, half, dtype=f))).astype(f)
    pos = np.concatenate([np.arange(SEQ), 2048 + np.tile(np.arange(ST), SB)]).astype(f)
    ang = (inv[:, None] * pos[None, :]).astype(f)
    rc = np.zeros((RH, P, RC))
    for h in range(RH):
        lg = np.log(1.0 - 2.0 ** (-5.0 - h))
        row, col = np.arange(P)[:, None], np.arange(384)[None, :]
        rc[h, :, :384] = np.where(col >= row, np.exp(lg * np.maximum(col - row, 0)), 0)
        rc[h, :NS, 384:416] = np.where(mine & (js <= is_), np.exp(lg * np.maximum(is_ - js, 0)), 0)
        of = np.arange(NS)[None, :] // ST == np.arange(SB)[:, None]
        rc[h, :, C_QD:C_KD] = (of * np.exp(lg * (np.arange(NS) % ST + 1))).reshape(-1)
        rc[h, :, C_KD] = np.exp(lg * (SEQ - 1 - np.arange(P)))
        rc[h, :, C_KD + 1] = np.exp(lg * (P - 1 - np.arange(P)))
        rc[h, :, C_KD + 2] = np.exp(lg * (ST - 1 - np.arange(P) % ST))
        rc[h, :, C_KD + 3] = np.exp(lg * ST)
    return {k: np.ascontiguousarray(v, dtype=f) for k, v in dict(
        mean_w=np.full((P, P), 1.0 / D), head_w=(j // N == i // N) / N, ident=np.eye(P),
        tri=tri, levels_m=lev, tri_s=np.stack([mine & (js < is_), mine & (js <= is_)], 1),
        own=np.arange(3 * NS)[:, None] % NS // ST == np.arange(SB)[None, :], blocks_m=(j // N == i // N),
        run_m=np.tile(run, (P, 1)), trig=np.stack([np.cos(ang), np.sin(ang)], 1), rc=rc).items()}


def kernel(**inputs):
    import concourse.bacc as bacc
    from concourse.bass_utils import run_bass_kernel_spmd

    a = {k: np.asarray(v) for k, v in inputs.items()}

    def columns(w, widths, blocks):
        k, m = w.shape
        u = w.reshape(k // P, P, m // widths, widths).transpose(2, 1, 0, 3)
        return u.reshape(m // widths, P, blocks, -1).transpose(0, 2, 1, 3)

    def gate_up(w):
        w = w[0].reshape(D, 2, 2, HALF)
        out = np.stack([np.concatenate([columns(w[:, n, f], 2 * P, 2) for n in range(2)], 1) for f in range(2)])
        return out

    def down(w):
        w = w[0].reshape(2, HALF, D)
        return np.stack([columns(w[f], 2 * P, 4).reshape(4, 8, P, -1) for f in range(2)])

    w_in = a["w_in"][0]
    q0, k0, v0, g0, s0 = 0, RH * DK, 2 * RH * DK, 2 * RH * DK + RH * DV, 2 * RH * DK + 2 * RH * DV
    l0 = s0 + 3 * RW
    gr0 = l0 + 128 + 160
    gw0 = gr0 + D
    mix = []
    for h in range(RH):
        steps = [columns(w_in[:, s0 + n * RW + h * 2 * P:s0 + n * RW + (h + 1) * 2 * P], 2 * P, 2)[0] for n in range(3)]
        for c0 in (q0, k0):
            w = w_in[:, c0 + h * DK:c0 + (h + 1) * DK]
            steps.append(columns(np.concatenate([w[:, 0::2], w[:, 1::2]], 1), 2 * P, 2)[0])
        for c0 in (v0, g0):
            w = w_in[:, c0 + h * DV:c0 + (h + 1) * DV]
            steps.append(columns(w[:, 0:2 * P], 2 * P, 2)[0])
            if c0 == v0:
                steps.append(columns(w[:, 2 * P:], 2 * P, 2)[0])
            else:
                steps += [columns(w[:, 2 * P:3 * P], P, 1)[0], columns(w[:, 3 * P:], P, 1)[0]]
        mix.append(np.concatenate(steps, 0))
    w_lora = columns(w_in[:, l0:l0 + 2 * P], 2 * P, 2)[0]
    w_lora2 = np.zeros((1, P, BLK), np.float32)
    w_lora2[0, :, :KT * GATE1] = columns(w_in[:, l0 + 2 * P:gr0], GATE1, 1)[0, 0]
    w_lora = np.concatenate([w_lora, w_lora2], 0)[None]
    w_gates = columns(w_in[:, gr0:], 2 * P, 2).reshape(-1, P, BLK)
    w_ro = columns(a["w_ret_o"][0], 2 * P, 2).reshape(4, 4, P, BLK)
    w_wo = columns(a["w_rwkv_o"][0], 2 * P, 1).reshape(4, 2, P, BLK)

    def tiles(v):
        return np.moveaxis(v.reshape(*v.shape[:-1], -1, P), (-1, -2), (0, 1))

    x = np.concatenate([a["x_prompt"].reshape(SEQ, D), a["x_sample"].reshape(NS, D)], 0)
    pp = np.zeros((PAIRS, P, PP), np.float32)
    pp[:, 0:64, 0:P] = a["rwkv_w_up"][0].reshape(64, PAIRS, P).transpose(1, 0, 2)
    pp[:, 64:P, 0:P] = a["rwkv_a_up"][0].reshape(64, PAIRS, P).transpose(1, 0, 2)
    gup = a["rwkv_g_up"][0].reshape(160, PAIRS, P).transpose(1, 0, 2)
    pp[:, :, P:2 * P] = gup[:, 0:P]
    pp[:, 0:GATE1, 2 * P:3 * P] = gup[:, P:]
    shift = a["state_shift"][0]
    pp[:, :, C_SHIFT:C_SHIFT + 3 * SB] = shift[:, :3 * RW].reshape(SB, 3, PAIRS, P).transpose(2, 3, 1, 0).reshape(PAIRS, P, 3 * SB)
    mu = a["rwkv_mu"][0]
    pp[:, :, C_MU:C_MU + 3] = mu[:3 * RW].reshape(3, PAIRS, P).transpose(1, 2, 0)
    for c, name in ((C_W0, "rwkv_w0"), (C_A0, "rwkv_a0"), (C_KK, "rwkv_k_k"), (C_KA, "rwkv_k_a"), (C_RK, "rwkv_r_k"),
                    (C_LNW, "rwkv_ln_w"), (C_LNB, "rwkv_ln_b")):
        pp[:, :, c] = a[name][0].reshape(PAIRS, P)
    lpk = np.zeros((P, 3 * SB + 3), np.float32)
    for k in range(3):
        c = 3 * RW + k * P
        n = min(P, mu.size - c)
        lpk[:n, k * SB:(k + 1) * SB] = shift[:, c:c + n].T
        lpk[:n, 3 * SB + k] = mu[c:c + n]
    gains = np.stack([tiles(a[n].reshape(-1)) for n in ("norm_ffn1", "norm_mix", "norm_ffn2", "norm_final")], 1)
    s_ret = a["state_ret"][0].reshape(SB, RH, P, 2, DV).transpose(1, 0, 2, 3, 4)
    s_rw = a["state_rwkv"][0].reshape(SB, PAIRS, 2, N, N).transpose(1, 2, 4, 0, 3).reshape(PAIRS, P, SB, N)
    arrays = dict(
        x=tiles(x), gu1=gate_up(a["ffn1_w_gu"]), gu2=gate_up(a["ffn2_w_gu"]), down1=down(a["ffn1_w_down"]),
        down2=down(a["ffn2_w_down"]), w_lora=w_lora, w_mix=np.stack(mix), w_gates=w_gates, w_ro=w_ro, w_wo=w_wo,
        w_out=columns(a["w_out"][0], 2 * P, 2).reshape(4, 4, P, BLK), gains=gains, pp=pp, lpk=lpk, s_ret=s_ret, s0=s_rw,
        **consts())
    outs = dict(y=(P, KT, T), ret_p=(RH, 2, P, DV), ret_s=(RH, SB, P, 2, DV), rwkv_p=(PAIRS, P, N),
                rwkv_s=(PAIRS, P, SB, N), last_lora=(P, 3, 1 + SB), last=(RH, P, 6, 1 + SB))
    nc = bacc.Bacc("TRN2", target_bir_lowering=False, num_devices=1)
    d, arrs = {}, {}
    for name, v in arrays.items():
        v = np.ascontiguousarray(v)
        arrs[f"in_{name}"] = v
        d[name] = nc.dram_tensor(f"in_{name}", v.shape, F32, kind="ExternalInput").ap()
    for name, shape in outs.items():
        d[name] = nc.dram_tensor(f"out_{name}", shape, F32, kind="ExternalOutput").ap()
    d["spill"] = nc.dram_tensor("spill", (P, KT, T), F32).ap()
    d["gates"] = nc.dram_tensor("gates", (2, PAIRS // 2, 2, P, 2, T), F32).ap()
    build(nc, d)
    r = run_bass_kernel_spmd(nc, [arrs], core_ids=[0]).results[0]
    o = {name: r[f"out_{name}"] for name in outs}
    y = o["y"].transpose(2, 1, 0).reshape(T, D)
    ret_p = o["ret_p"].transpose(0, 2, 1, 3).reshape(1, 1, RH, DK, DV)
    ret_s = o["ret_s"].reshape(RH, SB, DK, DV).transpose(1, 0, 2, 3)[None]
    rw_p = o["rwkv_p"].reshape(2 * PAIRS, N, N).transpose(0, 2, 1)[None, None]
    rw_s = o["rwkv_s"].reshape(PAIRS, 2, N, SB, N).transpose(3, 0, 1, 4, 2).reshape(1, SB, 2 * PAIRS, N, N)
    main = o["last"].reshape(RH, P, 3, 2, 1 + SB).transpose(4, 2, 0, 3, 1).reshape(1 + SB, 3 * RW)
    low = o["last_lora"].transpose(2, 1, 0).reshape(1 + SB, 3 * P)[:, :288]
    z = np.concatenate([main, low], 1)
    c = np.ascontiguousarray
    return (c(y[:SEQ].reshape(1, SEQ, D)), c(y[SEQ:].reshape(SB, ST, D)), c(ret_p), c(rw_p), c(z[None, 0:1]),
            c(ret_s), c(rw_s), c(z[None, 1:]))
```
